# Optimizing a Trainium2 kernel written in Bass

```python
import math
import jax, jax.numpy as jnp
from jax import lax
import numpy as np

D_MODEL = 1024
BATCH = 1
SEQ = 2048
DEPTH = 1

N_MEM = 256
GLA_HEADS = 4
GLA_DK = D_MODEL // 16
GLA_DV = D_MODEL // 8
GLA_RANK = 16
GLA_GATE_NORM = 16.0
GLA_CHUNK = 64
SB_HEADS = 4
SB_DH = D_MODEL // 16
SB_BLOCK = 128
SB_GROUPS = 8
MEM_HEADS = 4
MEM_DH = D_MODEL // 16
GLA_QK_W = GLA_HEADS * GLA_DK
GLA_V_W = GLA_HEADS * GLA_DV
SB_W = SB_HEADS * SB_DH
MEM_W = MEM_HEADS * MEM_DH
D_MIX = GLA_V_W + SB_W + MEM_W
SPLIT_NAMES = ("gla_q", "gla_k", "gla_v", "gla_gate", "gla_alpha",
               "sb_q", "sb_k", "sb_v", "sb_gate", "mem_q", "mem_gate")
SPLIT_SIZES = (GLA_QK_W, GLA_QK_W, GLA_V_W, GLA_V_W, GLA_RANK,
               SB_W, SB_W, SB_W, SB_W, MEM_W, MEM_W)
D_IN = 3088
ALPHA = (2.0 * DEPTH) ** 0.25
BETA = (8.0 * DEPTH) ** -0.25
LN_EPS = 1e-5
RMS_EPS = 1e-6

kernel_name = "gla_stickbreaking_memxattn_deepnorm_hybrid"

def _split_cols(proj):
    parts, off = [], 0
    for n in SPLIT_SIZES:
        parts.append(proj[..., off:off + n])
        off += n
    return parts

def _layer_norm(x, g, b):
    xf = x.astype(jnp.float32)
    mu = jnp.mean(xf, axis=-1, keepdims=True)
    var = jnp.mean(jnp.square(xf - mu), axis=-1, keepdims=True)
    return ((xf - mu) * lax.rsqrt(var + LN_EPS) * g + b).astype(x.dtype)

def _gla(q, k, v, log_a):
    B, T, H, dk = q.shape
    dv = v.shape[-1]
    n = T // GLA_CHUNK

    def to_chunks(t):
        return t.astype(jnp.float32).reshape(B, n, GLA_CHUNK, H, t.shape[-1]).transpose(1, 0, 3, 2, 4)

    qc = to_chunks(q) * (dk ** -0.5)
    kc, vc, gc = to_chunks(k), to_chunks(v), to_chunks(log_a)
    causal = jnp.asarray(np.tril(np.ones((GLA_CHUNK, GLA_CHUNK), dtype=bool)))

    def step(S, inp):
        qb, kb, vb, gb = inp
        G = jnp.cumsum(gb, axis=2)
        o_inter = jnp.einsum('bhck,bhkv->bhcv', qb * jnp.exp(G), S)
        diff = G[:, :, :, None, :] - G[:, :, None, :, :]
        decay = jnp.exp(jnp.where(causal[None, None, :, :, None], diff, -jnp.inf))
        A = jnp.einsum('bhik,bhjk,bhijk->bhij', qb, kb, decay)
        o_intra = jnp.einsum('bhij,bhjv->bhiv', A, vb)
        G_last = G[:, :, -1]
        k_dec = kb * jnp.exp(G_last[:, :, None, :] - G)
        S = jnp.exp(G_last)[..., None] * S + jnp.einsum('bhck,bhcv->bhkv', k_dec, vb)
        return S, o_inter + o_intra

    S0 = jnp.zeros((B, H, dk, dv), jnp.float32)
    _, o = lax.scan(step, S0, (qc, kc, vc, gc))
    return o.transpose(1, 0, 3, 2, 4).reshape(B, T, H, dv)

def _stick_breaking(q, k, v):
    B, T, H, d = q.shape
    nq = T // SB_BLOCK
    n_groups = math.gcd(nq, SB_GROUPS)
    gs = nq // n_groups
    qf = (q.astype(jnp.float32) * (d ** -0.5)).transpose(0, 2, 1, 3)
    kt = k.astype(jnp.float32).transpose(0, 2, 1, 3)
    vt = v.astype(jnp.float32).transpose(0, 2, 1, 3)
    tri_in = jnp.asarray(np.tril(np.ones((SB_BLOCK, SB_BLOCK), np.float32), -1))
    outs = []
    for g in range(n_groups):
        nb = (g + 1) * gs
        L = nb * SB_BLOCK
        k_g, v_g = kt[:, :, :L], vt[:, :, :L]
        tri_blk = jnp.asarray(np.tril(np.ones((nb, nb), np.float32), -1))
        key_pos = jnp.arange(L)
        q_g = qf[:, :, g * gs * SB_BLOCK:(g + 1) * gs * SB_BLOCK].reshape(
            B, H, gs, SB_BLOCK, d).transpose(2, 0, 1, 3, 4)
        starts = (g * gs + jnp.arange(gs, dtype=jnp.int32)) * SB_BLOCK

        def block(args, k_g=k_g, v_g=v_g, tri_blk=tri_blk, key_pos=key_pos, nb=nb, L=L):
            qblk, start = args
            z = jnp.einsum('bhqd,bhkd->bhqk', qblk, k_g)
            q_pos = start + jnp.arange(SB_BLOCK)
            mask = key_pos[None, :] < q_pos[:, None]
            lsn = jax.nn.log_sigmoid(-z)
            lf = jnp.where(mask, lsn, 0.0).reshape(B, H, SB_BLOCK, nb, SB_BLOCK)
            within = jnp.einsum('bhqnk,kj->bhqnj', lf, tri_in)
            across = jnp.einsum('bhqn,nm->bhqm', jnp.sum(lf, axis=-1), tri_blk)
            rest = (within + across[..., None]).reshape(B, H, SB_BLOCK, L)
            w = jnp.exp(jnp.where(mask, z + lsn + rest, -jnp.inf))
            return jnp.einsum('bhqk,bhkd->bhqd', w, v_g)

        o = lax.map(block, (q_g, starts))
        outs.append(o.transpose(1, 2, 0, 3, 4).reshape(B, H, gs * SB_BLOCK, d))
    o = jnp.concatenate(outs, axis=2)
    return o.transpose(0, 2, 1, 3).reshape(B, T, H * d)

def _mem_attn(q, mem, w_mkv):
    B, T, _ = q.shape
    kv = mem @ w_mkv
    km = kv[..., :MEM_W].reshape(B, N_MEM, MEM_HEADS, MEM_DH)
    vm = kv[..., MEM_W:].reshape(B, N_MEM, MEM_HEADS, MEM_DH)
    qh = q.reshape(B, T, MEM_HEADS, MEM_DH)
    s = jnp.einsum('bthd,bmhd->bhtm', qh, km).astype(jnp.float32) * (MEM_DH ** -0.5)
    p = jax.nn.softmax(s, axis=-1)
    o = jnp.einsum('bhtm,bmhd->bthd', p, vm.astype(jnp.float32))
    return o.reshape(B, T, MEM_W)

def _layer(x, mem, w_in, w_a2, b_a, gla_nw, w_mkv, w_out, ln_g, ln_b):
    B, T, _ = x.shape
    proj = x @ w_in
    gq, gk, gv, gg, ga, sq, sk, sv, sg, mq, mg = _split_cols(proj)
    log_a = jax.nn.log_sigmoid((ga @ w_a2 + b_a).astype(jnp.float32)) / GLA_GATE_NORM
    o_gla = _gla(gq.reshape(B, T, GLA_HEADS, GLA_DK), gk.reshape(B, T, GLA_HEADS, GLA_DK),
                 gv.reshape(B, T, GLA_HEADS, GLA_DV), log_a.reshape(B, T, GLA_HEADS, GLA_DK))
    o_gla = o_gla * lax.rsqrt(jnp.mean(jnp.square(o_gla), axis=-1, keepdims=True) + RMS_EPS) * gla_nw
    o_gla = o_gla.reshape(B, T, GLA_V_W)
    o_sb = _stick_breaking(sq.reshape(B, T, SB_HEADS, SB_DH), sk.reshape(B, T, SB_HEADS, SB_DH),
                           sv.reshape(B, T, SB_HEADS, SB_DH))
    o_mem = _mem_attn(mq, mem, w_mkv)
    mix = jnp.concatenate([o_gla * jax.nn.silu(gg.astype(jnp.float32)),
                           o_sb * jax.nn.silu(sg.astype(jnp.float32)),
                           o_mem * jax.nn.silu(mg.astype(jnp.float32))], axis=-1).astype(x.dtype)
    y = mix @ w_out
    return _layer_norm(ALPHA * x + y, ln_g, ln_b)

def setup_inputs(seed: int = 0) -> dict:
    key = jax.random.key(seed)
    ks = jax.random.split(key, 10)
    x = jax.random.normal(ks[0], (BATCH, SEQ, D_MODEL), jnp.float32)
    mem = jax.random.normal(ks[1], (BATCH, N_MEM, D_MODEL), jnp.float32)
    col_scale = np.full((D_IN,), D_MODEL ** -0.5, np.float32)
    off = 0
    for name, n in zip(SPLIT_NAMES, SPLIT_SIZES):
        if name in ("gla_v", "sb_v"):
            col_scale[off:off + n] *= BETA
        off += n
    w_in = jax.random.normal(ks[2], (DEPTH, D_MODEL, D_IN), jnp.float32) * jnp.asarray(col_scale)
    w_alpha2 = jax.random.normal(ks[3], (DEPTH, GLA_RANK, GLA_QK_W), jnp.float32) * GLA_RANK ** -0.5
    b_alpha = 0.1 * jax.random.normal(ks[4], (DEPTH, GLA_QK_W), jnp.float32)
    gla_norm_w = 1.0 + 0.02 * jax.random.normal(ks[5], (DEPTH, GLA_DV), jnp.float32)
    mkv_scale = np.concatenate([np.full((MEM_W,), D_MODEL ** -0.5, np.float32),
                                np.full((MEM_W,), D_MODEL ** -0.5 * BETA, np.float32)])
    w_mem_kv = jax.random.normal(ks[6], (DEPTH, D_MODEL, 2 * MEM_W), jnp.float32) * jnp.asarray(mkv_scale)
    w_out = jax.random.normal(ks[7], (DEPTH, D_MIX, D_MODEL), jnp.float32) * (D_MIX ** -0.5 * BETA)
    ln_g = 1.0 + 0.02 * jax.random.normal(ks[8], (DEPTH, D_MODEL), jnp.float32)
    ln_b = 0.02 * jax.random.normal(ks[9], (DEPTH, D_MODEL), jnp.float32)
    return {"x": x, "mem": mem, "w_in": w_in, "w_alpha2": w_alpha2, "b_alpha": b_alpha,
            "gla_norm_w": gla_norm_w, "w_mem_kv": w_mem_kv, "w_out": w_out,
            "ln_g": ln_g, "ln_b": ln_b}

def reference(x, mem, w_in, w_alpha2, b_alpha, gla_norm_w, w_mem_kv, w_out, ln_g, ln_b):
    for l in range(DEPTH):
        x = _layer(x, mem, w_in[l], w_alpha2[l], b_alpha[l], gla_norm_w[l], w_mem_kv[l],
                   w_out[l], ln_g[l], ln_b[l])
    return x


_drawn_inputs = setup_inputs


def setup_inputs(seed=0):
    import zlib

    import numpy as np

    out = dict(_drawn_inputs(seed))
    spreads = {}
    factors = {'mem': 6.657,
     'b_alpha': 6.255,
     'gla_norm_w': 43.02,
     'w_mem_kv': 5.744,
     'ln_g': 8.984,
     'ln_b': 8.555}
    for name, (base, spread) in spreads.items():
        noise = np.random.default_rng([zlib.crc32(name.encode()), seed]).standard_normal(out[name].shape)
        drawn = base * np.exp(spread * noise) if base else spread * noise
        out[name] = __import__('jax').numpy.asarray(drawn.astype(out[name].dtype))
    for name, factor in factors.items():
        out[name] = (out[name] * factor).astype(out[name].dtype)
    return out
```

```python
import concourse.bass as bass
from concourse import mybir
from concourse.alu_op_type import AluOpType as ALU
from contextlib import ExitStack

F32 = mybir.dt.float32
F32R = mybir.dt.float32r
I32 = mybir.dt.int32
ACT = mybir.ActivationFunctionType
AX = mybir.AxisListType
ds = bass.ds

P = 128
T = 2048
D = 1024
KC = D // P
NT = T // P
BANK = 512
N_MEM = 256
GLA_H, DK, DV, RANK = 4, 64, 128, 16
SB_H, DH = 4, 64
MEM_H = 4
SCALE = DH ** -0.5
ALPHA = 2.0 ** 0.25
LN_EPS, RMS_EPS = 1e-5, 1e-6
GQ, GK, GV, GG, GA = 0, 256, 512, 1024, 1536
SQ, SK, SV, SG, MQ, MG = 1552, 1808, 2064, 2320, 2576, 2832
D_IN = 3088
MIX_GLA, MIX_SB, MIX_MEM = 0, 512, 768


def make_identity(nc, ident):
    with ExitStack() as ctx:
        zeroed = ctx.enter_context(nc.semaphore("ident_zeroed"))
        made = ctx.enter_context(nc.semaphore("ident_made"))
        block = ctx.enter_context(nc.Block())

        @block.gpsimd
        def _(pool):
            nc.gpsimd.memset(ident[:], 0.0).then_inc(zeroed, 1)
            pool.wait_ge(zeroed, 1)
            nc.gpsimd.affine_select(out=ident[:], in_=ident[:], compare_op=ALU.not_equal, fill=1.0, base=0,
                                    pattern=[[-1, P]], channel_multiplier=1).then_inc(made, 1)
            pool.wait_ge(made, 1)


def project(nc, x, w_in, projT, ident):
    NC = T // BANK
    ROUNDS = 12
    SEGMENTS = [(6, GQ, SQ, False), (2, 768, MQ, False), (2, GG, SG, True), (2, GG + 256, MG, True)]
    XSLOTS, WSLOTS, NBANK = 2, 2, 8
    with ExitStack() as ctx:
        sb = lambda n, s, d=F32: ctx.enter_context(nc.sbuf_tensor(n, s, d))
        sem = lambda n: ctx.enter_context(nc.semaphore(n))
        x_in = sb("x_in", [P, XSLOTS, D])
        x_hi = sb("x_hi", [P, KC, T], F32R)
        x_lo = sb("x_lo", [P, KC, T], F32R)
        w_raw = sb("w_raw", [P, WSLOTS, KC, P])
        w_hi = sb("w_hi", [P, WSLOTS, KC, P], F32R)
        w_lo = sb("w_lo", [P, WSLOTS, KC, P], F32R)
        staged = sb("staged", [P, WSLOTS, T])
        acc = ctx.enter_context(nc.psum_tensor("acc", [P, NBANK, BANK], F32))
        x_loaded = [sem(f"x_loaded{s}") for s in range(XSLOTS)]
        x_turned = sem("x_turned")
        x_hi_done = sem("x_hi_done")
        x_split = sem("x_split")
        w_loaded = [sem(f"w_loaded{s}") for s in range(WSLOTS)]
        w_hi_done = sem("w_hi_done")
        w_split = sem("w_split")
        acc_ready = sem("acc_ready")
        evacuated = sem("evacuated")
        stored = [sem(f"stored{s}") for s in range(WSLOTS)]
        block = ctx.enter_context(nc.Block())
        w_cols = w_in[0].rearrange("(k p) c -> p k c", p=P)

        @block.sync
        def _(sp):
            for s in range(WSLOTS):
                sp.sem_inc(stored[s], 16)
            with sp.Fori(0, NT // XSLOTS) as it:
                for s in range(XSLOTS):
                    t = it * XSLOTS + s
                    sp.wait_ge(x_split, t + 1)
                    sp.dma_start(x_in[:, s], x[0, ds(t * P, P), :]).then_inc(x_loaded[s], 16)

            def load(col, g, s):
                sp.wait_ge(w_split, g + 1)
                sp.dma_start(w_raw[:, s], w_cols[:, :, ds(col, P)]).then_inc(w_loaded[s], 16)

            done = 0
            for rounds, col0, col1, _ in SEGMENTS:
                with sp.Fori(0, rounds) as it:
                    load(it * P + col0, it * 2 + 2 * done, 0)
                    load(it * P + col1, it * 2 + 2 * done + 1, 1)
                done += rounds
            load(GA, 2 * ROUNDS, 0)

        @block.gpsimd
        def _(pool):
            def round_group(it, s):
                pool.wait_ge(w_loaded[s], it * 16 + 16)
                pool.wait_ge(acc_ready, it * (2 * NC) + (s * NC + NC))
                pool.nop(nofuse=True)
                nc.gpsimd.tensor_copy(w_hi[:, s], w_raw[:, s]).then_inc(w_hi_done, 1)

            with pool.Fori(0, ROUNDS) as it:
                for s in range(WSLOTS):
                    round_group(it, s)
            round_group(ROUNDS, 0)

        @block.vector
        def _(dve):
            dve.sem_inc(x_split, XSLOTS)
            dve.sem_inc(w_split, WSLOTS)
            with dve.Fori(0, NT // XSLOTS) as it:
                for s in range(XSLOTS):
                    t = it * XSLOTS + s
                    dve.wait_ge(x_hi_done, t + 1)
                    turned = acc[:, 2 * s:2 * s + 2, :].rearrange("p b (k t) -> p (b k) t", t=P)
                    nc.vector.tensor_tensor(x_lo[:, :, ds(t * P, P)], turned,
                                            x_hi[:, :, ds(t * P, P)].bitcast(F32),
                                            ALU.subtract).then_inc(x_split, 1)

            def split_group(it, s):
                dve.wait_ge(w_hi_done, it * 2 + s + 1)
                nc.vector.tensor_tensor(w_lo[:, s], w_raw[:, s], w_hi[:, s].bitcast(F32),
                                        ALU.subtract).then_inc(w_split, 1)

            with dve.Fori(0, ROUNDS) as it:
                for s in range(WSLOTS):
                    split_group(it, s)
            split_group(ROUNDS, 0)

        @block.tensor
        def _(pe):
            pe.sem_inc(acc_ready, NBANK)
            with pe.Fori(0, NT // XSLOTS) as it:
                for s in range(XSLOTS):
                    pe.wait_ge(x_loaded[s], it * 16 + 16)
                    pe.wait_ge(x_split, it * XSLOTS + s + 1)
                    for k in range(KC):
                        last = nc.tensor.transpose(acc[:, 2 * s + k // 4, (k % 4) * P:(k % 4 + 1) * P],
                                                   x_in[:, s, k * P:(k + 1) * P], ident[:])
                    last.then_inc(x_turned, 1)
            pe.wait_ge(x_split, XSLOTS + NT)

            def group(it, s):
                pe.wait_ge(w_split, it * 2 + WSLOTS + s + 1)
                for c in range(NC):
                    pe.wait_ge(evacuated, it * (2 * NC) + (s * NC + c + 1))
                    bank = acc[:, s * NC + c, :]
                    for k in range(KC):
                        for n, (w, xs) in enumerate(((w_hi, x_hi), (w_hi, x_lo), (w_lo, x_hi))):
                            last = nc.tensor.matmul(bank, w[:, s, k, :], xs[:, k, c * BANK:(c + 1) * BANK],
                                                    start=(k == 0 and n == 0), stop=(k == KC - 1 and n == 2))
                    last.then_inc(acc_ready, 1)

            with pe.Fori(0, ROUNDS) as it:
                for s in range(WSLOTS):
                    group(it, s)
            group(ROUNDS, 0)

        @block.scalar
        def _(act):
            act.sem_inc(evacuated, NBANK)
            with act.Fori(0, NT // XSLOTS) as it:
                for s in range(XSLOTS):
                    t = it * XSLOTS + s
                    act.wait_ge(x_turned, t + 1)
                    turned = acc[:, 2 * s:2 * s + 2, :].rearrange("p b (k t) -> p (b k) t", t=P)
                    nc.scalar.activation(x_hi[:, :, ds(t * P, P)], turned, ACT.Copy).then_inc(x_hi_done, 1)

            def write_back(it, s, row, rows, func):
                act.wait_ge(stored[s], it * 16 + 16)
                for c in range(NC):
                    n = it * (2 * NC) + (s * NC + c)
                    act.wait_ge(acc_ready, n + NBANK + 1)
                    nc.scalar.activation(staged[:, s, c * BANK:(c + 1) * BANK], acc[:, s * NC + c, :],
                                         func).then_inc(evacuated, 1)
                act.wait_ge(evacuated, n + NBANK + 1)
                act.dma_start(projT[ds(row, rows), :], staged[0:rows, s, :]).then_inc(stored[s], 16)

            done = 0
            for rounds, col0, col1, gate in SEGMENTS:
                with act.Fori(0, rounds) as it:
                    write_back(it + done, 0, it * P + col0, P, ACT.Silu if gate else ACT.Copy)
                    write_back(it + done, 1, it * P + col1, P, ACT.Silu if gate else ACT.Copy)
                done += rounds
            write_back(ROUNDS, 0, GA, RANK, ACT.Copy)
            act.wait_ge(stored[0], 16 * (ROUNDS + 2))
            act.wait_ge(stored[1], 16 * (ROUNDS + 1))


def stick_breaking(nc, projT, mix, ident):
    PIECE, GROUP = 1024, 4
    pieces = []
    for i in range(NT):
        end = (i + 1) * P
        while end:
            first = (end - 1) // PIECE * PIECE
            pieces.append((i, first, end, end == (i + 1) * P))
            end = first
    groups = [(p, kb, min(GROUP, end // P - kb))
              for p, (_, first, end, _) in enumerate(pieces) for kb in range(first // P, end // P, GROUP)]
    NP, NG = len(pieces), len(groups)
    groups_of = [[g for g in range(NG) if groups[g][0] == p] for p in range(NP)]
    last_group = {pieces[groups[g][0]][0]: g for g in range(NG)}
    first_group = {pieces[groups[g][0]][0]: g for g in reversed(range(NG))}
    ZS, BS, SS, WS, OS = 2, 3, 2, 4, 2
    assert NP % (BS * ZS) == 0 and NG % WS == 0
    with ExitStack() as ctx:
        sb = lambda n, s, d=F32: ctx.enter_context(nc.sbuf_tensor(n, s, d))
        sem = lambda n: ctx.enter_context(nc.semaphore(n))
        k_raw = sb("k_raw", [P, T])
        k_hi = sb("k_hi", [P, T], F32R)
        k_lo = sb("k_lo", [P, T], F32R)
        q_raw = sb("q_raw", [P, T])
        q_both = sb("q_both", [P, T], F32R)
        v_raw = sb("v_raw", [DH, T])
        v_sb = sb("v_sb", [P, NT, DH])
        beta = sb("beta", [P, BS, PIECE])
        keep = sb("keep", [P, SS, PIECE])
        prod = sb("prod", [P, SS, PIECE + 1])
        wT = sb("wT", [P, WS, GROUP * P])
        zs = ctx.enter_context(nc.psum_tensor("zs", [P, ZS, PIECE], F32))
        tb = ctx.enter_context(nc.psum_tensor("tb", [P, 2, BANK], F32))
        ob = ctx.enter_context(nc.psum_tensor("ob", [P, OS, BANK], F32))
        raw_loaded = sem("raw_loaded")
        k_rounded, q_rounded = sem("k_rounded"), sem("q_rounded")
        head_split = sem("head_split")
        v_turned, v_ready = sem("v_turned"), sem("v_ready")
        z_ready = sem("z_ready")
        sig_done = sem("sig_done")
        masked = sem("masked")
        scanned = sem("scanned")
        w_done = sem("w_done")
        prod_set = sem("prod_set")
        w_turned = sem("w_turned")
        wt_act, wt_dve = sem("wt_act"), sem("wt_dve")
        av_done = sem("av_done")
        o_done = sem("o_done")
        block = ctx.enter_context(nc.Block())

        @block.sync
        def _(sp):
            with sp.Fori(0, SB_H) as h:
                sp.wait_ge(head_split, h + 1)
                sp.wait_ge(v_turned, h + 1)
                for half in range(2):
                    sp.dma_start(k_raw[half * DH:(half + 1) * DH, :],
                                 projT[ds(h * DH + SK, DH), :]).then_inc(raw_loaded, 16)
                    sp.dma_start(q_raw[half * DH:(half + 1) * DH, :],
                                 projT[ds(h * DH + SQ, DH), :]).then_inc(raw_loaded, 16)
                sp.dma_start(v_raw[:, :], projT[ds(h * DH + SV, DH), :]).then_inc(raw_loaded, 16)

        @block.gpsimd
        def _(pool):
            with pool.Fori(0, SB_H) as h:
                pool.wait_ge(raw_loaded, h * 80 + 80)
                pool.wait_ge(z_ready, h * NP + 1)
                pool.nop(nofuse=True)
                nc.gpsimd.tensor_copy(q_both[:, :], q_raw[:, :]).then_inc(q_rounded, 1)
                for p, (i, first, end, diagonal) in enumerate(pieces):
                    if not diagonal:
                        continue
                    pool.wait_ge(sig_done, h * NP + (ZS + p + 1))
                    pool.nop(nofuse=True)
                    off = i * P - first
                    for buf, slot, fill in ((beta, p % BS, 0.0), (keep, p % SS, 1.0)):
                        part = buf[:, slot, off:off + P]
                        last = nc.gpsimd.affine_select(out=part, in_=part, compare_op=ALU.is_gt, fill=fill, base=0,
                                                       pattern=[[-1, P]], channel_multiplier=1)
                    last.then_inc(masked, 1)

        @block.scalar
        def _(act):
            act.sem_inc(sig_done, ZS)
            act.sem_inc(wt_act, 1)
            with act.Fori(0, SB_H) as h:
                act.wait_ge(raw_loaded, h * 80 + 80)
                act.wait_ge(z_ready, h * NP + 1)
                nc.scalar.activation(k_hi[:, :], k_raw[:, :], ACT.Copy).then_inc(k_rounded, 1)
                act.wait_ge(v_turned, h + 2)
                act.wait_ge(av_done, h * NG + WS)
                nc.scalar.activation(v_sb[:, 0:NT // 2, :], tb[:, 0, :].rearrange("p (k d) -> p k d", d=DH),
                                     ACT.Copy).then_inc(v_ready, 1)

                def sigmoids(p):
                    n = pieces[p][2] - pieces[p][1]
                    act.wait_ge(z_ready, h * NP + (p + 2))
                    act.wait_ge(scanned, h * NP + (p + 1))
                    before = groups_of[p - BS][-1] + 1 if p >= BS else groups_of[p - BS][-1] + 1 - NG
                    act.wait_ge(w_turned, h * NG + (NG + before))
                    nc.scalar.activation(beta[:, p % BS, 0:n], zs[:, p % ZS, 0:n], ACT.Sigmoid, scale=SCALE)
                    nc.scalar.activation(keep[:, p % SS, 0:n], zs[:, p % ZS, 0:n], ACT.Sigmoid,
                                         scale=-SCALE).then_inc(sig_done, 1)

                sigmoids(0)
                sigmoids(1)
                for p in range(NP):
                    if p + 2 < NP:
                        sigmoids(p + 2)
                    for g in groups_of[p]:
                        if g % 2 == 0:
                            n = groups[g][2] * P
                            act.wait_ge(w_turned, h * NG + (NG + g + 1))
                            act.wait_ge(av_done, h * NG + (g + 1))
                            nc.scalar.activation(wT[:, g % WS, 0:n], tb[:, 0, 0:n], ACT.Copy).then_inc(wt_act, 1)

        @block.vector
        def _(dve):
            dve.sem_inc(scanned, SS)
            dve.sem_inc(head_split, 1)
            dve.sem_inc(wt_dve, 1)
            dve.sem_inc(o_done, OS)
            nc.vector.memset(prod[:, :, :], 1.0).then_inc(prod_set, 1)
            dve.wait_ge(prod_set, 1)
            with dve.Fori(0, SB_H) as h:
                dve.wait_ge(k_rounded, h + 1)
                nc.vector.tensor_tensor(k_lo[:, :], k_raw[:, :], k_hi[:, :].bitcast(F32), ALU.subtract)
                dve.wait_ge(q_rounded, h + 1)
                nc.vector.tensor_tensor(q_both[DH:P, :], q_raw[DH:P, :], q_both[DH:P, :].bitcast(F32),
                                        ALU.subtract).then_inc(head_split, 1)
                dve.wait_ge(v_turned, h + 2)
                dve.wait_ge(av_done, h * NG + WS)
                nc.vector.tensor_copy(v_sb[:, NT // 2:NT, :],
                                      tb[:, 1, :].rearrange("p (k d) -> p k d", d=DH)).then_inc(v_ready, 1)

                def weights(p):
                    i, first, end, diagonal = pieces[p]
                    n = end - first
                    if diagonal:
                        dve.wait_ge(masked, h * NT + (i + 1))
                        initial = 1.0
                    else:
                        dve.wait_ge(sig_done, h * NP + (ZS + p + 1))
                        dve.wait_ge(scanned, h * NP + (SS + p))
                        initial = prod[:, (p - 1) % SS, 0:1]
                        nc.vector.tensor_copy(prod[:, p % SS, n:n + 1], initial)
                    s = keep[:, p % SS, 0:n][:, ::-1]
                    nc.vector.tensor_tensor_scan(prod[:, p % SS, 0:n][:, ::-1], s, s, initial,
                                                 ALU.mult, ALU.bypass).then_inc(scanned, 1)
                    dve.wait_ge(scanned, h * NP + (SS + p + 1))
                    nc.vector.tensor_tensor(beta[:, p % BS, 0:n], beta[:, p % BS, 0:n],
                                            prod[:, p % SS, 1:n + 1], ALU.mult).then_inc(w_done, 1)

                def finish(i):
                    dve.wait_ge(av_done, h * NG + (WS + last_group[i] + 1))
                    nc.vector.tensor_copy(mix[:, i, ds(h * DH + MIX_SB, DH)], ob[:, i % OS, 0:DH]).then_inc(o_done, 1)

                weights(0)
                for p in range(NP):
                    if p + 1 < NP:
                        weights(p + 1)
                    for g in groups_of[p]:
                        if g % 2 == 1:
                            n = groups[g][2] * P
                            dve.wait_ge(w_turned, h * NG + (NG + g + 1))
                            dve.wait_ge(av_done, h * NG + (g + 1))
                            nc.vector.tensor_copy(wT[:, g % WS, 0:n], tb[:, 1, 0:n]).then_inc(wt_dve, 1)
                    if p and pieces[p - 1][1] == 0:
                        finish(pieces[p - 1][0])
                finish(NT - 1)

        @block.tensor
        def _(pe):
            pe.sem_inc(w_turned, NG)
            pe.sem_inc(v_turned, 1)
            pe.sem_inc(z_ready, 1)
            pe.sem_inc(av_done, WS)
            with pe.Fori(0, SB_H) as h:
                pe.wait_ge(raw_loaded, h * 80 + 80)
                pe.wait_ge(wt_act, h * (NG // 2) + 1)
                pe.wait_ge(wt_dve, h * (NG // 2) + 1)
                pe.nop(nofuse=True)
                for kb in range(NT):
                    last = nc.tensor.transpose(tb[:, kb // 8, kb % 8 * DH:(kb % 8 + 1) * DH],
                                               v_raw[:, kb * P:(kb + 1) * P], ident[0:DH, 0:DH])
                last.then_inc(v_turned, 1)
                pe.wait_ge(head_split, h + 2)

                def scores(p):
                    i, first, end, _ = pieces[p]
                    pe.wait_ge(sig_done, h * NP + (p + 1))
                    for c in range(first, end, BANK):
                        n = min(BANK, end - c)
                        out = zs[:, p % ZS, c - first:c - first + n]
                        nc.tensor.matmul(out, q_both[:, i * P:(i + 1) * P], k_hi[:, c:c + n], start=True, stop=False)
                        last = nc.tensor.matmul(out, q_both[:, i * P:(i + 1) * P], k_lo[:, c:c + n],
                                                start=False, stop=True)
                    last.then_inc(z_ready, 1)

                def product(g):
                    p, kb0, n = groups[g]
                    i = pieces[p][0]
                    copied = wt_act if g % 2 == 0 else wt_dve
                    pe.wait_ge(copied, h * (NG // 2) + (g // 2 + 2))
                    if g == first_group[i]:
                        pe.wait_ge(o_done, h * NT + (i + 1))
                    for j in range(n):
                        last = nc.tensor.matmul(ob[:, i % OS, 0:DH], wT[:, g % WS, j * P:(j + 1) * P],
                                                v_sb[:, kb0 + j, :], start=(g == first_group[i] and j == 0),
                                                stop=(g == last_group[i] and j == n - 1))
                    last.then_inc(av_done, 1)

                scores(0)
                scores(1)
                pe.wait_ge(v_ready, h * 2 + 2)
                for g, (p, kb0, n) in enumerate(groups):
                    if g == groups_of[p][0]:
                        if p + 2 < NP:
                            scores(p + 2)
                        pe.wait_ge(w_done, h * NP + (p + 1))
                    copied = wt_act if g % 2 == 0 else wt_dve
                    pe.wait_ge(copied, h * (NG // 2) + (g // 2 + 1))
                    first = pieces[p][1]
                    for j in range(n):
                        off = (kb0 + j) * P - first
                        last = nc.tensor.transpose(tb[:, g % 2, j * P:(j + 1) * P],
                                                   beta[:, p % BS, off:off + P], ident[:])
                    last.then_inc(w_turned, 1)
                    if g:
                        product(g - 1)
                product(NG - 1)


def gla(nc, projT, w_alpha2, b_alpha, mix, squares, ident):
    LEVELS = [64, 32, 16, 8, 4, 2, 1]
    NL = len(LEVELS)
    TO_END, FROM_START, NF = NL, NL + 1, NL + 2
    PAIR = GLA_H // 2
    W = PAIR * P
    LA_C = BANK
    with ExitStack() as ctx:
        sb = lambda n, s, d=F32: ctx.enter_context(nc.sbuf_tensor(n, s, d))
        sem = lambda n: ctx.enter_context(nc.semaphore(n))
        low = sb("low", [RANK, T])
        w2 = sb("w2", [RANK, GLA_H * DK])
        b2 = sb("b2", [P, PAIR])
        logit = sb("logit", [P, PAIR, T])
        soft = sb("soft", [P, PAIR, T])
        gsum = sb("gsum", [P, PAIR, T])
        within = sb("within", [P, T])
        level_mask = sb("level_mask", [P, NL, GLA_H * P // 2])
        eye = sb("eye", [P, GLA_H * P])
        qk = sb("qk", [P, 2, 2 * W])
        vT = sb("vT", [P, 2, GLA_H, P])
        v_sb = sb("gv_sb", [P, 2, GLA_H * DV])
        fac = sb("fac", [P, 2, NF, W])
        m = sb("m", [P, 2, NF, W])
        kd = sb("kd", [P, 2, W])
        att = sb("att", [P, 2, GLA_H, P])
        state = sb("state", [P, 2, PAIR, DV])
        sq = sb("sq", [P, 2, GLA_H, DV])
        lev = ctx.enter_context(nc.psum_tensor("lev", [P, 5, BANK], F32))
        o_ps = ctx.enter_context(nc.psum_tensor("o_ps", [P, BANK], F32))
        v_ps = ctx.enter_context(nc.psum_tensor("v_ps", [P, BANK], F32))
        kd_ps = ctx.enter_context(nc.psum_tensor("kd_ps", [P, BANK], F32))
        st_ps = lev[:, 3, BANK // 2:BANK]
        in_loaded = sem("in_loaded")
        logit_ready, logit_sum = sem("logit_ready"), sem("logit_sum")
        pre_act, pre_dve, pre_pool = sem("pre_act"), sem("pre_dve"), sem("pre_pool")
        tile_loaded = [sem(f"tile_loaded{s}") for s in range(2)]
        g_copied = sem("g_copied")
        abs_done = sem("abs_done")
        eye_done = sem("eye_done")
        half_done = sem("half_done")
        diffs_done = sem("diffs_done")
        fac_done = sem("fac_done")
        m_done = sem("m_done")
        turned = sem("turned")
        nat_done = sem("nat_done")
        lev_ready = sem("lev_ready")
        overlaid = sem("overlaid")
        o_ready = sem("o_ready")
        o_out = sem("o_out")
        st_ready = sem("st_ready")
        st_done = sem("st_done")
        block = ctx.enter_context(nc.Block())

        def blocks(ap, c):
            return ap.rearrange("p (n h c) -> p n h c", h=2, c=c)

        def roles(s, c):
            v = qk[:, s, :]
            return bass.AP(v.tensor, v.offset, [list(v.ap[0]), [2 * c, W // (2 * c)], [W + c, 2], [1, c]])

        @block.sync
        def _(sp):
            sp.dma_start(low[:, :], projT[GA:GA + RANK, :]).then_inc(in_loaded, 16)
            sp.dma_start(w2[:, :], w_alpha2[0]).then_inc(in_loaded, 16)
            with nc.allow_non_contiguous_dma(reason="256 biases, once"):
                sp.dma_start(b2[:, :], b_alpha[0].rearrange("(a p) -> p a", p=P)).then_inc(in_loaded, 16)
            with sp.Fori(0, NT // 2) as it:
                for s in range(2):
                    t = it * 2 + s
                    sp.wait_ge(m_done, t + 1)
                    sp.nop(nofuse=True)
                    sp.wait_ge(nat_done, t + 1)
                    sp.nop(nofuse=True)
                    sp.wait_ge(lev_ready, t * 5 + 1)
                    for at, row in ((0, GK), (W, GQ)):
                        sp.dma_start(qk[:, s, at:at + W].rearrange("p (a t) -> p a t", t=P),
                                     projT[row:row + W, ds(t * P, P)].rearrange("(a p) t -> p a t", p=P)
                                     ).then_inc(tile_loaded[s], 16)
                    sp.dma_start(vT[:, s], projT[GV:GV + GLA_H * DV, ds(t * P, P)].rearrange("(h p) t -> p h t", p=P)
                                 ).then_inc(tile_loaded[s], 16)

        @block.gpsimd
        def _(pool):
            nc.gpsimd.memset(level_mask[:, :, :], 1.0).then_inc(pre_pool, 1)
            nc.gpsimd.memset(att[:, :, :, :], 0.0).then_inc(pre_pool, 1)
            nc.gpsimd.memset(state[:, 0], 0.0).then_inc(pre_pool, 1)
            pool.wait_ge(pre_pool, 3)
            n = 3
            for l, c in enumerate(LEVELS):
                for base, sign in ((0, 1), (c - 1, -1)):
                    view = level_mask[:, l, :].rearrange("p (h b r) -> p h b r", h=GLA_H, r=c)
                    nc.gpsimd.affine_select(out=view, in_=view, compare_op=ALU.is_ge, fill=0.0, base=base,
                                            pattern=[[0, GLA_H], [-2 * c * sign, P // (2 * c)], [0, c]],
                                            channel_multiplier=sign).then_inc(pre_pool, 1)
                    n += 1
                    pool.wait_ge(pre_pool, n)
            with pool.Fori(0, NT // 2) as it:
                for s in range(2):
                    t = it * 2 + s
                    pool.wait_ge(g_copied, t + 1)
                    g = fac[:, s, FROM_START, :]
                    for l, c in enumerate(LEVELS):
                        gm = blocks(g, c)[:, :, 0:1, c - 1:c].rearrange("p n a b -> p n (a b)")
                        view = lambda ap: ap.rearrange("p (n c) -> p n c", c=2 * c)
                        nc.gpsimd.tensor_tensor(view(fac[:, s, l, :]), view(g),
                                                gm.to_broadcast([P, W // (2 * c), 2 * c]), ALU.subtract)
                    view = lambda ap: ap.rearrange("p (n c) -> p n c", c=P)
                    nc.gpsimd.tensor_tensor(view(fac[:, s, TO_END, :]), view(g),
                                            view(g)[:, :, P - 1:P].to_broadcast([P, PAIR, P]),
                                            ALU.subtract).then_inc(diffs_done, 1)

        @block.scalar
        def _(act):
            act.sem_inc(nat_done, 2)
            act.sem_inc(o_out, 2)
            act.wait_ge(in_loaded, 48)
            for a in range(PAIR):
                for c in range(T // LA_C):
                    n = a * (T // LA_C) + c
                    act.wait_ge(logit_ready, n + 1)
                    nc.scalar.activation(logit[:, a, c * LA_C:(c + 1) * LA_C], lev[:, n % 2, :], ACT.Identity,
                                         bias=b2[:, a:a + 1]).then_inc(logit_sum, 1)
            act.wait_ge(logit_sum, PAIR * T // LA_C)
            nc.scalar.activation(soft[:, :, :], logit[:, :, :], ACT.Abs).then_inc(pre_act, 1)
            act.wait_ge(pre_act, 1)
            nc.scalar.activation(soft[:, :, :], soft[:, :, :], ACT.Exp, scale=-1.0).then_inc(pre_act, 1)
            act.wait_ge(pre_act, 2)
            nc.scalar.activation(soft[:, :, :], soft[:, :, :], ACT.Ln, bias=1.0).then_inc(pre_act, 1)
            act.wait_ge(pre_dve, 5)

            def factors(t, s):
                act.wait_ge(m_done, t + 1)
                act.wait_ge(st_done, t + 1)
                nc.scalar.activation(fac[:, s, FROM_START, :].rearrange("p (a t) -> p a t", t=P),
                                     gsum[:, :, ds(t * P, P)], ACT.Copy).then_inc(g_copied, 1)
                act.wait_ge(diffs_done, t + 1)
                nc.scalar.activation(fac[:, s], fac[:, s], ACT.Abs).then_inc(abs_done, 1)
                act.wait_ge(abs_done, t + 1)
                nc.scalar.activation(fac[:, s], fac[:, s], ACT.Exp, scale=-1.0).then_inc(fac_done, 1)

            def natural(t, s):
                act.wait_ge(turned, t + 1)
                act.wait_ge(st_ready, t + 1)
                nc.scalar.activation(v_sb[:, s, :], v_ps[:, :], ACT.Copy)
                nc.scalar.activation(kd[:, s, :], kd_ps[:, 0:W], ACT.Copy).then_inc(nat_done, 1)

            def finish(t, s, it):
                act.wait_ge(o_ready, t + 2)
                act.wait_ge(o_out, t + 1)
                o_mix = mix[:, ds(t, 1), MIX_GLA:MIX_GLA + GLA_H * DV].rearrange("p a c -> p (a c)")
                nc.scalar.activation(o_mix, o_ps[:, :], ACT.Copy, scale=SCALE)
                for h in range(GLA_H):
                    last = nc.scalar.activation(sq[:, s, h, :], o_ps[:, h * DV:(h + 1) * DV], ACT.Square, scale=SCALE,
                                                accum_out=squares[:, s, ds(it, 1), h:h + 1].rearrange("p a b -> p (a b)"))
                last.then_inc(o_out, 1)

            factors(0, 0)
            with act.Fori(0, NT // 2 - 1) as it:
                for s in range(2):
                    natural(it * 2 + s, s)
                    factors(it * 2 + s + 1, 1 - s)
                    finish(it * 2 + s, s, it)
            natural(NT - 2, 0)
            factors(NT - 1, 1)
            finish(NT - 2, 0, NT // 2 - 1)
            natural(NT - 1, 1)
            finish(NT - 1, 1, NT // 2 - 1)

        @block.vector
        def _(dve):
            dve.sem_inc(m_done, 2)
            dve.sem_inc(overlaid, NL + 1)
            dve.sem_inc(st_done, 2)
            nc.vector.memset(within[:, :], 1.0).then_inc(pre_dve, 1)
            dve.wait_ge(pre_dve, 1)
            nc.vector.memset(within[:, :].rearrange("p (n c) -> p n c", c=P)[:, :, 0:1], 0.0).then_inc(pre_dve, 1)
            for h in range(GLA_H):
                nc.vector.tensor_copy(eye[:, h * P:(h + 1) * P], ident[:, :]).then_inc(eye_done, 1)
            dve.wait_ge(pre_act, 3)
            nc.vector.tensor_scalar(logit[:, :, :], logit[:, :, :], 0.0, None, ALU.min).then_inc(pre_dve, 1)
            dve.wait_ge(pre_dve, 3)
            nc.vector.tensor_tensor(soft[:, :, :], logit[:, :, :], soft[:, :, :], ALU.subtract).then_inc(pre_dve, 1)
            dve.wait_ge(pre_dve, 4)
            nc.vector.tensor_scalar(soft[:, :, :], soft[:, :, :], 1.0 / 16.0, None, ALU.mult).then_inc(pre_act, 1)
            dve.wait_ge(pre_act, 4)
            for a in range(PAIR):
                last = nc.vector.tensor_tensor_scan(gsum[:, a, :], within[:, :], soft[:, a, :], 0.0, ALU.mult, ALU.add)
            last.then_inc(pre_dve, 1)

            def multiply(t, s):
                dve.wait_ge(fac_done, t + 1)
                dve.wait_ge(tile_loaded[s], (t - s) * 24 + 48)
                dve.wait_ge(o_ready, t)
                for l, c in enumerate(LEVELS):
                    nc.vector.tensor_tensor(blocks(m[:, s, l, :], c), roles(s, c), blocks(fac[:, s, l, :], c), ALU.mult)
                nc.vector.tensor_tensor(m[:, s, TO_END, :], qk[:, s, 0:W], fac[:, s, TO_END, :], ALU.mult)
                nc.vector.tensor_tensor(m[:, s, FROM_START, :], qk[:, s, W:2 * W], fac[:, s, FROM_START, :],
                                        ALU.mult).then_inc(m_done, 1)

            def overlay(t, s):
                for l, c in enumerate(LEVELS):
                    dve.wait_ge(lev_ready, t * 5 + (6 + l // 2 + 1))
                    dve.wait_ge(overlaid, t * (NL + 1) + (NL + 1 + l))
                    dve.nop(nofuse=True)
                    out = att[:, s].rearrange("p h (b u r) -> p h b u r", u=2, r=c)[:, :, :, 1, :]
                    shape = "p (h b r) -> p h b r"
                    nc.vector.copy_predicated(out, level_mask[:, l, :].bitcast(I32).rearrange(shape, h=GLA_H, r=c),
                                              lev[:, l // 2, (l % 2) * W:(l % 2 + 1) * W].rearrange(shape, h=GLA_H, r=c)
                                              ).then_inc(overlaid, 1)
                dve.wait_ge(lev_ready, t * 5 + 11)
                dve.wait_ge(overlaid, t * (NL + 1) + (2 * NL + 1))
                dve.nop(nofuse=True)
                nc.vector.copy_predicated(att[:, s], eye[:, :].bitcast(I32).rearrange("p (h t) -> p h t", t=P),
                                          lev[:, 4, :].rearrange("p (h t) -> p h t", t=P)).then_inc(overlaid, 1)
                dve.wait_ge(st_ready, t + 2)
                for a in range(PAIR):
                    last = nc.vector.scalar_tensor_tensor(state[:, 1 - s, a, :], state[:, s, a, :],
                                                          fac[:, s, FROM_START, a * P + P - 1:a * P + P],
                                                          st_ps[:, a * DV:(a + 1) * DV], ALU.mult, ALU.add)
                last.then_inc(st_done, 1)

            dve.wait_ge(pre_pool, 3 + 2 * NL)
            dve.wait_ge(eye_done, GLA_H)
            dve.wait_ge(fac_done, 1)
            dve.wait_ge(tile_loaded[0], 48)
            multiply_first(nc, m, qk, fac, blocks, roles, LEVELS, W).then_inc(m_done, 1)
            with dve.Fori(0, NT // 2 - 1) as it:
                multiply(it * 2 + 1, 1)
                overlay(it * 2, 0)
                multiply(it * 2 + 2, 0)
                overlay(it * 2 + 1, 1)
            multiply(NT - 1, 1)
            overlay(NT - 2, 0)
            overlay(NT - 1, 1)

        @block.tensor
        def _(pe):
            for n in range(PAIR * T // LA_C):
                a, c = n // (T // LA_C), n % (T // LA_C)
                if n == 0:
                    pe.wait_ge(in_loaded, 48)
                if n >= 2:
                    pe.wait_ge(logit_sum, n - 1)
                nc.tensor.matmul(lev[:, n % 2, :], w2[:, a * P:(a + 1) * P], low[:, c * LA_C:(c + 1) * LA_C],
                                 start=True, stop=True).then_inc(logit_ready, 1)
            pe.wait_ge(logit_sum, PAIR * T // LA_C)
            pe.wait_ge(pre_pool, 3)
            pe.sem_inc(lev_ready, 6)
            pe.sem_inc(st_ready, 1)
            pe.sem_inc(o_ready, 1)
            with pe.Fori(0, NT // 2) as it:
                for s in range(2):
                    t = it * 2 + s
                    pe.wait_ge(m_done, t + 3)
                    pe.wait_ge(nat_done, t + 2)
                    for h in range(GLA_H):
                        nc.tensor.transpose(v_ps[:, h * DV:(h + 1) * DV], vT[:, s, h, :], ident[:])
                    for a in range(PAIR):
                        last = nc.tensor.transpose(kd_ps[:, a * P:(a + 1) * P],
                                                   m[:, s, TO_END, a * P:(a + 1) * P], ident[:])
                    last.then_inc(turned, 1)
                    halves = 0
                    for banks in ((0, 1), (2, 3, 4)):
                        for odd in range(2):
                            for b in banks:
                                if not odd:
                                    pe.wait_ge(overlaid, t * (NL + 1) + min(2 * b + 2, NL + 1))
                                    if b == 3:
                                        pe.wait_ge(st_done, t + 2)
                                else:
                                    pe.wait_ge(half_done, t * 6 + (b + 1))
                                for l in range(2 * b, min(2 * b + 2, NL)) if b < 4 else (NL,):
                                    for h in range(odd, GLA_H, 2):
                                        rows, a = slice(odd * DK, odd * DK + DK), h // 2
                                        if l == NL:
                                            last = nc.tensor.matmul(
                                                lev[:, 4, h * P:(h + 1) * P], qk[rows, s, a * P:(a + 1) * P],
                                                qk[rows, s, W + a * P:W + (a + 1) * P], start=True, stop=True)
                                            continue
                                        c = LEVELS[l]
                                        mine = m[rows, s, l, a * P:(a + 1) * P]
                                        at = (l % 2) * W + h * (P // 2)
                                        last = nc.tensor.matmul(
                                            lev[:, b, at:at + P // 2].rearrange("p (b r) -> p b r", r=c), mine,
                                            mine.rearrange("p (b u r) -> p b u r", u=2, r=c)[:, :, 1, :],
                                            start=True, stop=True)
                                last.then_inc(lev_ready if odd else half_done, 1)
                    pe.wait_ge(o_out, t + 2)
                    pe.wait_ge(nat_done, t + 3)
                    pe.wait_ge(overlaid, (t + 2) * (NL + 1))
                    pe.wait_ge(st_done, t + 2)
                    for h in (0, 2, 1, 3):
                        rows, a = slice(h % 2 * DK, h % 2 * DK + DK), h // 2
                        if h == 1:
                            pe.wait_ge(half_done, t * 6 + 6)
                        nc.tensor.matmul(o_ps[:, h * DV:(h + 1) * DV], m[rows, s, FROM_START, a * P:(a + 1) * P],
                                         state[rows, s, a, :], start=True, stop=False)
                        last = nc.tensor.matmul(o_ps[:, h * DV:(h + 1) * DV], att[:, s, h, :],
                                                v_sb[:, s, h * DV:(h + 1) * DV], start=False, stop=True)
                        if h == 2:
                            last.then_inc(half_done, 1)
                    last.then_inc(o_ready, 1)
                    for h in range(GLA_H):
                        rows, a = slice(h % 2 * DK, h % 2 * DK + DK), h // 2
                        last = nc.tensor.matmul(st_ps[rows, a * DV:(a + 1) * DV], kd[:, s, a * P + h % 2 * DK:a * P + h % 2 * DK + DK],
                                                v_sb[:, s, h * DV:(h + 1) * DV], start=True, stop=True)
                    last.then_inc(st_ready, 1)


def multiply_first(nc, m, qk, fac, blocks, roles, levels, width):
    nl = len(levels)
    for l, c in enumerate(levels):
        nc.vector.tensor_tensor(blocks(m[:, 0, l, :], c), roles(0, c), blocks(fac[:, 0, l, :], c), ALU.mult)
    nc.vector.tensor_tensor(m[:, 0, nl, :], qk[:, 0, 0:width], fac[:, 0, nl, :], ALU.mult)
    return nc.vector.tensor_tensor(m[:, 0, nl + 1, :], qk[:, 0, width:2 * width], fac[:, 0, nl + 1, :], ALU.mult)


def memory(nc, mem, w_kv, projT, mix, ident):
    MB = N_MEM // P
    HW = MEM_H * DH
    with ExitStack() as ctx:
        sb = lambda n, s, d=F32: ctx.enter_context(nc.sbuf_tensor(n, s, d))
        sem = lambda n: ctx.enter_context(nc.semaphore(n))
        mem_in = sb("mem_in", [P, MB, D])
        memT = sb("memT", [P, KC, N_MEM])
        w_sb = sb("w_sb", [P, KC, 2 * HW])
        kmT = sb("kmT", [P, 2, N_MEM])
        vm = sb("vm", [P, MB, HW])
        mq = sb("mq", [P, 2, 2, P])
        top = sb("top", [P, 2, MEM_H])
        probs = sb("probs", [P, 2, MEM_H, N_MEM])
        total = sb("total", [P, 2, MEM_H])
        inverse = sb("inverse", [P, 2, MEM_H])
        probsT = sb("probsT", [P, 2, MEM_H * MB, P])
        s_ps = ctx.enter_context(nc.psum_tensor("s_ps", [P, 2, 2 * BANK], F32))
        t_ps = ctx.enter_context(nc.psum_tensor("t_ps", [P, 2, BANK], F32))
        o_ps = ctx.enter_context(nc.psum_tensor("mo_ps", [P, 2, BANK], F32))
        loaded, memT_ps, memT_done = sem("loaded"), sem("memT_ps"), sem("memT_done")
        kv_ps, kv_done = sem("kv_ps"), sem("kv_done")
        q_loaded = [sem(f"q_loaded{s}") for s in range(2)]
        s_ready = sem("s_ready")
        max_done, top_done = sem("max_done"), sem("top_done")
        exp_done = sem("exp_done")
        p_turned = sem("p_turned")
        pt_act, pt_dve = sem("pt_act"), sem("pt_dve")
        o_ready = sem("mo_ready")
        inv_done = sem("inv_done")
        o_done = sem("mo_done")
        block = ctx.enter_context(nc.Block())

        def place(h):
            return h % 2 * 2 + h // 2

        @block.sync
        def _(sp):
            sp.dma_start(mem_in[:, :, :], mem[0].rearrange("(b p) d -> p b d", p=P)).then_inc(loaded, 16)
            sp.dma_start(w_sb[:, :, :], w_kv[0].rearrange("(k p) c -> p k c", p=P)).then_inc(loaded, 16)
            with sp.Fori(0, NT // 2) as it:
                for s in range(2):
                    t = it * 2 + s
                    sp.wait_ge(s_ready, t + 1)
                    sp.dma_start(mq[:, s], projT[MQ:MQ + HW, ds(t * P, P)].rearrange("(a p) t -> p a t", p=P)
                                 ).then_inc(q_loaded[s], 16)

        @block.tensor
        def _(pe):
            pe.sem_inc(s_ready, 2)
            pe.sem_inc(p_turned, 2)
            pe.sem_inc(o_ready, 2)
            pe.wait_ge(loaded, 32)
            for b in range(MB):
                for k in range(KC):
                    last = nc.tensor.transpose(s_ps[:, b, k * P:(k + 1) * P], mem_in[:, b, k * P:(k + 1) * P], ident[:])
            last.then_inc(memT_ps, 1)
            pe.wait_ge(memT_done, 2)
            for a in range(2):
                for k in range(KC):
                    nc.tensor.matmul(t_ps[:, a, 0:N_MEM], w_sb[:, k, a * P:(a + 1) * P], memT[:, k, :],
                                     start=(k == 0), stop=(k == KC - 1))
            for b in range(MB):
                for k in range(KC):
                    last = nc.tensor.matmul(o_ps[:, b, 0:HW], memT[:, k, b * P:(b + 1) * P], w_sb[:, k, HW:2 * HW],
                                            start=(k == 0), stop=(k == KC - 1))
            last.then_inc(kv_ps, 1)
            pe.wait_ge(kv_done, 2)

            def scores(n, s, it):
                pe.wait_ge(q_loaded[s], it * 16 + 16)
                pe.wait_ge(exp_done, n + 1)
                for h in range(MEM_H):
                    rows, a = slice(h % 2 * DH, h % 2 * DH + DH), h // 2
                    last = nc.tensor.matmul(s_ps[:, s, place(h) * N_MEM:(place(h) + 1) * N_MEM], mq[rows, s, a, :], kmT[rows, a, :],
                                            start=True, stop=True)
                last.then_inc(s_ready, 1)

            def products(n, s):
                pe.wait_ge(exp_done, n + 3)
                pe.wait_ge(pt_act, n + 1)
                pe.wait_ge(pt_dve, n + 1)
                for j in range(MEM_H * MB):
                    last = nc.tensor.transpose(t_ps[:, j // 4, j % 4 * P:(j % 4 + 1) * P],
                                               probs[:, s, j // MB, j % MB * P:(j % MB + 1) * P], ident[:])
                last.then_inc(p_turned, 1)
                pe.wait_ge(pt_act, n + 2)
                pe.wait_ge(pt_dve, n + 2)
                pe.wait_ge(o_done, n + 1)
                for j in range(MEM_H * MB):
                    h, b = j // MB, j % MB
                    last = nc.tensor.matmul(o_ps[:, s, h * DH:(h + 1) * DH], probsT[:, s, j, :], vm[:, b, h * DH:(h + 1) * DH],
                                            start=(b == 0), stop=(b == MB - 1))
                last.then_inc(o_ready, 1)

            scores(0, 0, 0)
            with pe.Fori(0, NT // 2 - 1) as it:
                scores(it * 2 + 1, 1, it)
                products(it * 2, 0)
                scores(it * 2 + 2, 0, it + 1)
                products(it * 2 + 1, 1)
            scores(NT - 1, 1, NT // 2 - 1)
            products(NT - 2, 0)
            products(NT - 1, 1)

        @block.scalar
        def _(act):
            act.sem_inc(exp_done, 2)
            act.sem_inc(pt_act, 1)
            act.wait_ge(memT_ps, 1)
            nc.scalar.activation(memT[:, :, 0:P], s_ps[:, 0, :].rearrange("p (k t) -> p k t", t=P),
                                 ACT.Copy).then_inc(memT_done, 1)
            act.wait_ge(kv_ps, 1)
            nc.scalar.activation(kmT[:, :, :], t_ps[:, :, 0:N_MEM], ACT.Copy).then_inc(kv_done, 1)

            def exps(n, s):
                act.wait_ge(top_done, n + 1)
                act.wait_ge(p_turned, n + 1)
                act.wait_ge(o_done, n + 1)
                for h in range(MEM_H):
                    last = nc.scalar.activation(probs[:, s, h, :], s_ps[:, s, place(h) * N_MEM:(place(h) + 1) * N_MEM], ACT.Exp,
                                                bias=top[:, s, place(h):place(h) + 1], scale=SCALE, accum_out=total[:, s, h:h + 1])
                last.then_inc(exp_done, 1)

            def copy_out(n, s):
                act.wait_ge(p_turned, n + 3)
                act.wait_ge(o_ready, n + 1)
                nc.scalar.activation(probsT[:, s, 0:4, :], t_ps[:, 0, :].rearrange("p (j t) -> p j t", t=P),
                                     ACT.Copy).then_inc(pt_act, 1)

            exps(0, 0)
            with act.Fori(0, NT // 2 - 1) as it:
                exps(it * 2 + 1, 1)
                copy_out(it * 2, 0)
                exps(it * 2 + 2, 0)
                copy_out(it * 2 + 1, 1)
            exps(NT - 1, 1)
            copy_out(NT - 2, 0)
            copy_out(NT - 1, 1)

        @block.vector
        def _(dve):
            dve.sem_inc(pt_dve, 1)
            dve.sem_inc(o_done, 2)
            dve.wait_ge(memT_ps, 1)
            nc.vector.tensor_copy(memT[:, :, P:2 * P], s_ps[:, 1, :].rearrange("p (k t) -> p k t", t=P)
                                  ).then_inc(memT_done, 1)
            dve.wait_ge(kv_ps, 1)
            nc.vector.tensor_copy(vm[:, :, :], o_ps[:, :, 0:HW]).then_inc(kv_done, 1)

            def maxima(n, s):
                dve.wait_ge(s_ready, n + 3)
                dve.wait_ge(exp_done, n + 1)
                nc.vector.reduce_max(top[:, s, :], s_ps[:, s, :].rearrange("p (h m) -> p h m", m=N_MEM),
                                     AX.X).then_inc(max_done, 1)
                dve.wait_ge(max_done, n + 1)
                nc.vector.tensor_scalar(top[:, s, :], top[:, s, :], -SCALE, None, ALU.mult).then_inc(top_done, 1)

            def finish(n, s):
                dve.wait_ge(p_turned, n + 3)
                dve.wait_ge(o_ready, n + 1)
                nc.vector.tensor_copy(probsT[:, s, 4:8, :], t_ps[:, 1, :].rearrange("p (j t) -> p j t", t=P)
                                      ).then_inc(pt_dve, 1)
                nc.vector.reciprocal(inverse[:, s, :], total[:, s, :]).then_inc(inv_done, 1)
                dve.wait_ge(inv_done, n + 1)
                dve.wait_ge(o_ready, n + 3)
                out = mix[:, ds(n, 1), MIX_MEM:MIX_MEM + HW].rearrange("p a (h d) -> p (a h) d", d=DH)
                nc.vector.tensor_tensor(out, o_ps[:, s, 0:HW].rearrange("p (h d) -> p h d", d=DH),
                                        inverse[:, s, :].rearrange("p (h a) -> p h a", a=1).to_broadcast([P, MEM_H, DH]),
                                        ALU.mult).then_inc(o_done, 1)

            maxima(0, 0)
            with dve.Fori(0, NT // 2 - 1) as it:
                maxima(it * 2 + 1, 1)
                finish(it * 2, 0)
                maxima(it * 2 + 2, 0)
                finish(it * 2 + 1, 1)
            maxima(NT - 1, 1)
            finish(NT - 2, 0)
            finish(NT - 1, 1)


def output(nc, x, w_out, gla_nw, ln_g, ln_b, projT, mix, squares, ident, out):
    GLA_C, CW = GLA_H, P
    with ExitStack() as ctx:
        sb = lambda n, s, d=F32: ctx.enter_context(nc.sbuf_tensor(n, s, d))
        sem = lambda n: ctx.enter_context(nc.semaphore(n))
        w_raw = sb("wo_raw", [P, 2, D])
        w_hi = sb("wo_hi", [P, KC, D], F32R)
        w_lo = sb("wo_lo", [P, KC, D], F32R)
        nw = sb("nw", [P, 1])
        ln_w = sb("ln_w", [P, D])
        ln_c = sb("ln_c", [P, D])
        rms = sb("rms", [P, 2, NT // 2, GLA_H])
        eps = sb("eps", [P, 2])
        gate = sb("gate", [P, 2, KC, P])
        x_sb = sb("x_sb", [P, 2, D])
        gated = sb("gated", [P, 2, KC, P])
        g_hi = sb("g_hi", [P, 2, KC, P], F32R)
        g_lo = sb("g_lo", [P, 2, KC, P], F32R)
        y = sb("y", [P, 2, D])
        stats = sb("stats", [P, 2, 2, 6])
        mean_var = sb("mean_var", [P, 2, 2])
        rstd = sb("rstd", [P, 2])
        t_ps = ctx.enter_context(nc.psum_tensor("gt_ps", [P, 2, 2, BANK], F32))
        y_ps = ctx.enter_context(nc.psum_tensor("y_ps", [P, 2, 2, BANK], F32))
        small_loaded = sem("small_loaded")
        wo_loaded = [sem(f"wo_loaded{s}") for s in range(2)]
        wo_rounded, wo_split = sem("wo_rounded"), sem("wo_split")
        rms_ln, rms_done, normed = sem("rms_ln"), sem("rms_done"), sem("normed")
        eps_set = sem("eps_set")
        tile_loaded = [sem(f"xg_loaded{s}") for s in range(2)]
        mt_ready = sem("mt_ready")
        gated_done = sem("gated_done")
        hi_done = sem("g_hi_done")
        lo_done = sem("g_lo_done")
        y_ready = sem("y_ready")
        sum_done = sem("sum_done")
        dve_step = sem("dve_step")
        ln_done, rstd_done = sem("ln_done"), sem("rstd_done")
        scaled, weighted, final = sem("scaled"), sem("weighted"), sem("final")
        out_stored = [sem(f"out_stored{s}") for s in range(2)]
        block = ctx.enter_context(nc.Block())

        @block.sync
        def _(sp):
            for s in range(2):
                sp.sem_inc(out_stored[s], 16)
            with nc.allow_non_contiguous_dma(reason="128 weights, once"):
                sp.dma_start(nw[:, :], gla_nw[0].rearrange("(p a) -> p a", a=1)).then_inc(small_loaded, 16)
            sp.dma_start(ln_w[:, :], ln_g[0].partition_broadcast(P)).then_inc(small_loaded, 16)
            sp.dma_start(ln_c[:, :], ln_b[0].partition_broadcast(P)).then_inc(small_loaded, 16)
            for k in range(KC):
                if k >= 2:
                    sp.wait_ge(wo_split, k - 1)
                sp.dma_start(w_raw[:, k % 2], w_out[0, k * P:(k + 1) * P, :]).then_inc(wo_loaded[k % 2], 16)
            with sp.Fori(0, NT // 2) as it:
                for s in range(2):
                    t = it * 2 + s
                    sp.wait_ge(gated_done, t + 1)
                    sp.wait_ge(sum_done, t + 1)
                    sp.dma_start(x_sb[:, s], x[0, ds(t * P, P), :]).then_inc(tile_loaded[s], 16)
                    for c0, cn, row in ((0, 4, GG), (4, 2, SG), (6, 2, MG)):
                        sp.dma_start(gate[:, s, c0:c0 + cn],
                                     projT[row:row + cn * P, ds(t * P, P)].rearrange("(c p) t -> p c t", p=P)
                                     ).then_inc(tile_loaded[s], 16)

        @block.gpsimd
        def _(pool):
            for k in range(KC):
                pool.wait_ge(wo_loaded[k % 2], (k // 2 + 1) * 16)
                nc.gpsimd.tensor_copy(w_hi[:, k, :], w_raw[:, k % 2, :]).then_inc(wo_rounded, 1)
            pool.wait_ge(rms_done, 3)
            for n in range(NT * GLA_H):
                t, h = n // GLA_H, n % GLA_H
                part = mix[:, t, h * DV:(h + 1) * DV]
                last = nc.gpsimd.tensor_scalar(part, part, rms[:, t % 2, t // 2, h:h + 1], None, ALU.mult)
                if h == GLA_H - 1:
                    last.then_inc(normed, 1)
            pool.wait_ge(small_loaded, 48)
            with pool.Fori(0, NT // 2) as it:
                for s in range(2):
                    t = it * 2 + s
                    pool.wait_ge(scaled, t + 1)
                    nc.gpsimd.tensor_tensor(y[:, s, :], y[:, s, :], ln_w[:, :], ALU.mult).then_inc(weighted, 1)

        @block.scalar
        def _(act):
            act.wait_ge(eps_set, 2)
            nc.scalar.activation(rms[:, :, :, :], squares[:, :, :, :], ACT.Ln, bias=eps[:, 0:1],
                                 scale=1.0 / DV).then_inc(rms_done, 1)
            act.wait_ge(rms_done, 1)
            nc.scalar.activation(rms[:, :, :, :], rms[:, :, :, :], ACT.Exp, scale=-0.5).then_inc(rms_done, 2)

            def round_gated(t, s):
                act.wait_ge(gated_done, t + 3)
                act.wait_ge(y_ready, t + 1)
                nc.scalar.activation(g_hi[:, s], gated[:, s], ACT.Copy).then_inc(hi_done, 1)

            def deviation(t, s):
                act.wait_ge(dve_step, t * 2 + 2)
                nc.scalar.activation(rstd[:, s:s + 1], mean_var[:, s, 1:2], ACT.Ln, bias=eps[:, 1:2]).then_inc(ln_done, 1)
                act.wait_ge(ln_done, t + 1)
                nc.scalar.activation(rstd[:, s:s + 1], rstd[:, s:s + 1], ACT.Exp, scale=-0.5).then_inc(rstd_done, 1)

            def store(t, s):
                act.wait_ge(final, t + 1)
                act.dma_start(out[0, ds(t * P, P), :], y[:, s, :]).then_inc(out_stored[s], 16)

            round_gated(0, 0)
            with act.Fori(0, NT // 2 - 1) as it:
                round_gated(it * 2 + 1, 1)
                deviation(it * 2, 0)
                store(it * 2, 0)
                round_gated(it * 2 + 2, 0)
                deviation(it * 2 + 1, 1)
                store(it * 2 + 1, 1)
            round_gated(NT - 1, 1)
            for s in range(2):
                deviation(NT - 2 + s, s)
                store(NT - 2 + s, s)
            for s in range(2):
                act.wait_ge(out_stored[s], 16 * (NT // 2 + 1))

        @block.vector
        def _(dve):
            dve.sem_inc(gated_done, 2)
            dve.sem_inc(sum_done, 2)
            nc.vector.memset(eps[:, 0:1], RMS_EPS).then_inc(eps_set, 1)
            nc.vector.memset(eps[:, 1:2], LN_EPS).then_inc(eps_set, 1)
            for k in range(KC):
                dve.wait_ge(wo_rounded, k + 1)
                nc.vector.tensor_tensor(w_lo[:, k, :], w_raw[:, k % 2, :], w_hi[:, k, :].bitcast(F32),
                                        ALU.subtract).then_inc(wo_split, 1)
            dve.wait_ge(small_loaded, 48)

            def gating(t, s, it):
                dve.wait_ge(mt_ready, t + 1)
                dve.wait_ge(tile_loaded[s], it * 64 + 64)
                parts = t_ps[:, s].rearrange("p b (c t) -> p (b c) t", t=P)
                nc.vector.scalar_tensor_tensor(gated[:, s, 0:GLA_C, :], parts[:, 0:GLA_C, :], nw[:, 0:1],
                                               gate[:, s, 0:GLA_C, :], ALU.mult, ALU.mult)
                nc.vector.tensor_tensor(gated[:, s, GLA_C:KC, :], parts[:, GLA_C:KC, :], gate[:, s, GLA_C:KC, :],
                                        ALU.mult).then_inc(gated_done, 1)
                dve.wait_ge(hi_done, t + 1)
                nc.vector.tensor_tensor(g_lo[:, s], gated[:, s], g_hi[:, s].bitcast(F32), ALU.subtract).then_inc(lo_done, 1)

            def layer_norm(t, s, it):
                dve.wait_ge(y_ready, t + 3)
                dve.wait_ge(out_stored[s], it * 16 + 16)
                nc.vector.scalar_tensor_tensor(y[:, s, :], x_sb[:, s, :], ALPHA,
                                               y_ps[:, s].rearrange("p b c -> p (b c)"), ALU.mult, ALU.add).then_inc(sum_done, 1)
                dve.wait_ge(sum_done, t + 3)
                for c in range(2):
                    last = nc.vector.bn_stats(stats[:, s, c, :], y[:, s, c * BANK:(c + 1) * BANK])
                last.then_inc(dve_step, 1)
                dve.wait_ge(dve_step, t * 2 + 1)
                dve.nop(nofuse=True)
                nc.vector.bn_aggr(mean_var[:, s, :], stats[:, s].rearrange("p c k -> p (c k)")).then_inc(dve_step, 1)

            def normalise(t, s):
                dve.wait_ge(rstd_done, t + 1)
                nc.vector.tensor_scalar(y[:, s, :], y[:, s, :], mean_var[:, s, 0:1], rstd[:, s:s + 1],
                                        ALU.subtract, ALU.mult).then_inc(scaled, 1)
                dve.wait_ge(weighted, t + 1)
                nc.vector.tensor_tensor(y[:, s, :], y[:, s, :], ln_c[:, :], ALU.add).then_inc(final, 1)

            gating(0, 0, 0)
            with dve.Fori(0, NT // 2 - 1) as it:
                gating(it * 2 + 1, 1, it)
                layer_norm(it * 2, 0, it)
                normalise(it * 2, 0)
                gating(it * 2 + 2, 0, it + 1)
                layer_norm(it * 2 + 1, 1, it)
                normalise(it * 2 + 1, 1)
            gating(NT - 1, 1, NT // 2 - 1)
            for s in range(2):
                layer_norm(NT - 2 + s, s, NT // 2 - 1)
                normalise(NT - 2 + s, s)

        @block.tensor
        def _(pe):
            pe.sem_inc(y_ready, 2)

            def turn(t, s):
                pe.wait_ge(normed, t + 1)
                pe.wait_ge(gated_done, t + 1)
                turn_tile(nc, t_ps, mix, t, s, ident).then_inc(mt_ready, 1)

            def multiply(t, s):
                pe.wait_ge(lo_done, t + 1)
                pe.wait_ge(sum_done, t + 1)
                for c in range(2):
                    for k in range(KC):
                        for n, (g, w) in enumerate(((g_hi, w_hi), (g_hi, w_lo), (g_lo, w_hi))):
                            last = nc.tensor.matmul(y_ps[:, s, c, :], g[:, s, k, :], w[:, k, c * BANK:(c + 1) * BANK],
                                                    start=(k == 0 and n == 0), stop=(k == KC - 1 and n == 2))
                last.then_inc(y_ready, 1)

            turn(0, 0)
            pe.wait_ge(wo_split, KC)
            for t in range(NT):
                if t + 1 < NT:
                    turn(t + 1, (t + 1) % 2)
                multiply(t, t % 2)


def turn_tile(nc, t_ps, mix, t, s, ident):
    for c in range(KC):
        last = nc.tensor.transpose(t_ps[:, s, c // 4, c % 4 * P:(c % 4 + 1) * P], mix[:, t, c * P:(c + 1) * P], ident[:])
    return last


def hybrid_layer(nc, x, mem, w_in, w_alpha2, b_alpha, gla_norm_w, w_mem_kv, w_out, ln_g, ln_b, out, stages=(1, 2, 3, 4, 5)):
    projT = nc.dram_tensor("projT", (D_IN, T), F32).ap()
    with ExitStack() as ctx:
        ident = ctx.enter_context(nc.sbuf_tensor("ident", [P, P], F32))
        make_identity(nc, ident)
        if 1 in stages:
            project(nc, x, w_in, projT, ident)
        mix = ctx.enter_context(nc.sbuf_tensor("mix", [P, NT, D], F32))
        squares = ctx.enter_context(nc.sbuf_tensor("squares", [P, 2, NT // 2, GLA_H], F32))
        if 2 in stages:
            stick_breaking(nc, projT, mix, ident)
        if 3 in stages:
            gla(nc, projT, w_alpha2, b_alpha, mix, squares, ident)
        if 4 in stages:
            memory(nc, mem, w_mem_kv, projT, mix, ident)
        if 5 in stages:
            output(nc, x, w_out, gla_norm_w, ln_g, ln_b, projT, mix, squares, ident, out)


INPUTS = ["x", "mem", "w_in", "w_alpha2", "b_alpha", "gla_norm_w", "w_mem_kv", "w_out", "ln_g", "ln_b"]


def kernel(**inputs):
    import numpy as np
    import concourse.bacc as bacc
    from concourse.bass_utils import run_bass_kernel_spmd

    nc = bacc.Bacc("TRN2", target_bir_lowering=False, num_devices=1)
    arrays, args = {}, []
    for name in INPUTS:
        a = np.ascontiguousarray(inputs[name])
        arrays[f"in_{name}"] = a
        args.append(nc.dram_tensor(f"in_{name}", a.shape, mybir.dt.from_np(a.dtype), kind="ExternalInput").ap())
    out = nc.dram_tensor("out", (1, T, D), F32, kind="ExternalOutput").ap()
    hybrid_layer(nc, *args, out)
    result = run_bass_kernel_spmd(nc, [arrays], core_ids=[0])
    return result.results[0]["out"]
```

```python
import concourse.bass as bass
from concourse import mybir
from concourse.alu_op_type import AluOpType as ALU
from contextlib import ExitStack

F32 = mybir.dt.float32
F32R = mybir.dt.float32r
I32 = mybir.dt.int32
ACT = mybir.ActivationFunctionType
AX = mybir.AxisListType
ds = bass.ds

P = 128
T = 2048
D = 1024
KC = D // P
NT = T // P
BANK = 512
N_MEM = 256
GLA_H, DK, DV, RANK = 4, 64, 128, 16
SB_H, DH = 4, 64
MEM_H = 4
SCALE = DH ** -0.5
ALPHA = 2.0 ** 0.25
LN_EPS, RMS_EPS = 1e-5, 1e-6
GQ, GK, GV, GG, GA = 0, 256, 512, 1024, 1536
SQ, SK, SV, SG, MQ, MG = 1552, 1808, 2064, 2320, 2576, 2832
D_IN = 3088
MIX_GLA, MIX_SB, MIX_MEM = 0, 512, 768


def make_identity(nc, ident):
    with ExitStack() as ctx:
        zeroed = ctx.enter_context(nc.semaphore("ident_zeroed"))
        made = ctx.enter_context(nc.semaphore("ident_made"))
        block = ctx.enter_context(nc.Block())

        @block.gpsimd
        def _(pool):
            nc.gpsimd.memset(ident[:], 0.0).then_inc(zeroed, 1)
            pool.wait_ge(zeroed, 1)
            nc.gpsimd.affine_select(out=ident[:], in_=ident[:], compare_op=ALU.not_equal, fill=1.0, base=0,
                                    pattern=[[-1, P]], channel_multiplier=1).then_inc(made, 1)
            pool.wait_ge(made, 1)


def project(nc, x, w_in, projT, ident):
    NC = T // BANK
    ROUNDS = 12
    SEGMENTS = [(6, GQ, SQ, False), (2, 768, MQ, False), (2, GG, SG, True), (2, GG + 256, MG, True)]
    XSLOTS, WSLOTS, NBANK = 2, 2, 8
    with ExitStack() as ctx:
        sb = lambda n, s, d=F32: ctx.enter_context(nc.sbuf_tensor(n, s, d))
        sem = lambda n: ctx.enter_context(nc.semaphore(n))
        x_in = sb("x_in", [P, XSLOTS, D])
        x_hi = sb("x_hi", [P, KC, T], F32R)
        x_lo = sb("x_lo", [P, KC, T], F32R)
        w_raw = sb("w_raw", [P, WSLOTS, KC, P])
        w_hi = sb("w_hi", [P, WSLOTS, KC, P], F32R)
        w_lo = sb("w_lo", [P, WSLOTS, KC, P], F32R)
        staged = sb("staged", [P, WSLOTS, T])
        acc = ctx.enter_context(nc.psum_tensor("acc", [P, NBANK, BANK], F32))
        x_loaded = [sem(f"x_loaded{s}") for s in range(XSLOTS)]
        x_turned = sem("x_turned")
        x_hi_done = sem("x_hi_done")
        x_split = sem("x_split")
        w_loaded = [sem(f"w_loaded{s}") for s in range(WSLOTS)]
        w_hi_done = sem("w_hi_done")
        w_split = sem("w_split")
        acc_ready = sem("acc_ready")
        evacuated = sem("evacuated")
        stored = [sem(f"stored{s}") for s in range(WSLOTS)]
        block = ctx.enter_context(nc.Block())
        w_cols = w_in[0].rearrange("(k p) c -> p k c", p=P)

        @block.sync
        def _(sp):
            for s in range(WSLOTS):
                sp.sem_inc(stored[s], 16)
            with sp.Fori(0, NT // XSLOTS) as it:
                for s in range(XSLOTS):
                    t = it * XSLOTS + s
                    sp.wait_ge(x_split, t + 1)
                    sp.dma_start(x_in[:, s], x[0, ds(t * P, P), :]).then_inc(x_loaded[s], 16)

            def load(col, g, s):
                sp.wait_ge(w_split, g + 1)
                sp.dma_start(w_raw[:, s], w_cols[:, :, ds(col, P)]).then_inc(w_loaded[s], 16)

            done = 0
            for rounds, col0, col1, _ in SEGMENTS:
                with sp.Fori(0, rounds) as it:
                    load(it * P + col0, it * 2 + 2 * done, 0)
                    load(it * P + col1, it * 2 + 2 * done + 1, 1)
                done += rounds
            load(GA, 2 * ROUNDS, 0)

        @block.gpsimd
        def _(pool):
            def round_group(it, s):
                pool.wait_ge(w_loaded[s], it * 16 + 16)
                pool.wait_ge(acc_ready, it * (2 * NC) + (s * NC + NC))
                pool.nop(nofuse=True)
                nc.gpsimd.tensor_copy(w_hi[:, s], w_raw[:, s]).then_inc(w_hi_done, 1)

            with pool.Fori(0, ROUNDS) as it:
                for s in range(WSLOTS):
                    round_group(it, s)
            round_group(ROUNDS, 0)

        @block.vector
        def _(dve):
            dve.sem_inc(x_split, XSLOTS)
            dve.sem_inc(w_split, WSLOTS)
            with dve.Fori(0, NT // XSLOTS) as it:
                for s in range(XSLOTS):
                    t = it * XSLOTS + s
                    dve.wait_ge(x_hi_done, t + 1)
                    turned = acc[:, 2 * s:2 * s + 2, :].rearrange("p b (k t) -> p (b k) t", t=P)
                    nc.vector.tensor_tensor(x_lo[:, :, ds(t * P, P)], turned,
                                            x_hi[:, :, ds(t * P, P)].bitcast(F32),
                                            ALU.subtract).then_inc(x_split, 1)

            def split_group(it, s):
                dve.wait_ge(w_hi_done, it * 2 + s + 1)
                nc.vector.tensor_tensor(w_lo[:, s], w_raw[:, s], w_hi[:, s].bitcast(F32),
                                        ALU.subtract).then_inc(w_split, 1)

            with dve.Fori(0, ROUNDS) as it:
                for s in range(WSLOTS):
                    split_group(it, s)
            split_group(ROUNDS, 0)

        @block.tensor
        def _(pe):
            pe.sem_inc(acc_ready, NBANK)
            with pe.Fori(0, NT // XSLOTS) as it:
                for s in range(XSLOTS):
                    pe.wait_ge(x_loaded[s], it * 16 + 16)
                    pe.wait_ge(x_split, it * XSLOTS + s + 1)
                    for k in range(KC):
                        last = nc.tensor.transpose(acc[:, 2 * s + k // 4, (k % 4) * P:(k % 4 + 1) * P],
                                                   x_in[:, s, k * P:(k + 1) * P], ident[:])
                    last.then_inc(x_turned, 1)
            pe.wait_ge(x_split, XSLOTS + NT)

            def group(it, s):
                pe.wait_ge(w_split, it * 2 + WSLOTS + s + 1)
                for c in range(NC):
                    pe.wait_ge(evacuated, it * (2 * NC) + (s * NC + c + 1))
                    bank = acc[:, s * NC + c, :]
                    for k in range(KC):
                        for n, (w, xs) in enumerate(((w_hi, x_hi), (w_hi, x_lo), (w_lo, x_hi))):
                            last = nc.tensor.matmul(bank, w[:, s, k, :], xs[:, k, c * BANK:(c + 1) * BANK],
                                                    start=(k == 0 and n == 0), stop=(k == KC - 1 and n == 2))
                    last.then_inc(acc_ready, 1)

            with pe.Fori(0, ROUNDS) as it:
                for s in range(WSLOTS):
                    group(it, s)
            group(ROUNDS, 0)

        @block.scalar
        def _(act):
            act.sem_inc(evacuated, NBANK)
            with act.Fori(0, NT // XSLOTS) as it:
                for s in range(XSLOTS):
                    t = it * XSLOTS + s
                    act.wait_ge(x_turned, t + 1)
                    turned = acc[:, 2 * s:2 * s + 2, :].rearrange("p b (k t) -> p (b k) t", t=P)
                    nc.scalar.activation(x_hi[:, :, ds(t * P, P)], turned, ACT.Copy).then_inc(x_hi_done, 1)

            def write_back(it, s, row, rows, func):
                act.wait_ge(stored[s], it * 16 + 16)
                for c in range(NC):
                    n = it * (2 * NC) + (s * NC + c)
                    act.wait_ge(acc_ready, n + NBANK + 1)
                    nc.scalar.activation(staged[:, s, c * BANK:(c + 1) * BANK], acc[:, s * NC + c, :],
                                         func).then_inc(evacuated, 1)
                act.wait_ge(evacuated, n + NBANK + 1)
                act.dma_start(projT[ds(row, rows), :], staged[0:rows, s, :]).then_inc(stored[s], 16)

            done = 0
            for rounds, col0, col1, gate in SEGMENTS:
                with act.Fori(0, rounds) as it:
                    write_back(it + done, 0, it * P + col0, P, ACT.Silu if gate else ACT.Copy)
                    write_back(it + done, 1, it * P + col1, P, ACT.Silu if gate else ACT.Copy)
                done += rounds
            write_back(ROUNDS, 0, GA, RANK, ACT.Copy)
            act.wait_ge(stored[0], 16 * (ROUNDS + 2))
            act.wait_ge(stored[1], 16 * (ROUNDS + 1))


def stick_breaking(nc, projT, sb_out, ident):
    PIECE, GROUP = 1024, 4
    pieces = []
    for i in range(NT):
        end = (i + 1) * P
        while end:
            first = (end - 1) // PIECE * PIECE
            pieces.append((i, first, end, end == (i + 1) * P))
            end = first
    groups = [(p, kb, min(GROUP, end // P - kb))
              for p, (_, first, end, _) in enumerate(pieces) for kb in range(first // P, end // P, GROUP)]
    NP, NG = len(pieces), len(groups)
    groups_of = [[g for g in range(NG) if groups[g][0] == p] for p in range(NP)]
    last_group = {pieces[groups[g][0]][0]: g for g in range(NG)}
    first_group = {pieces[groups[g][0]][0]: g for g in reversed(range(NG))}
    ZS, BS, SS, WS, OS = 2, 3, 2, 4, 2
    assert NP % (BS * ZS) == 0 and NG % WS == 0
    with ExitStack() as ctx:
        sb = lambda n, s, d=F32: ctx.enter_context(nc.sbuf_tensor(n, s, d))
        sem = lambda n: ctx.enter_context(nc.semaphore(n))
        k_raw = sb("k_raw", [P, T])
        k_hi = sb("k_hi", [P, T], F32R)
        k_lo = sb("k_lo", [P, T], F32R)
        q_raw = sb("q_raw", [P, T])
        q_both = sb("q_both", [P, T], F32R)
        v_raw = sb("v_raw", [DH, T])
        v_sb = sb("v_sb", [P, NT, DH])
        beta = sb("beta", [P, BS, PIECE])
        keep = sb("keep", [P, SS, PIECE])
        prod = sb("prod", [P, SS, PIECE + 1])
        wT = sb("wT", [P, WS, GROUP * P])
        head_out = sb("head_out", [P, NT, DH])
        zs = ctx.enter_context(nc.psum_tensor("zs", [P, ZS, PIECE], F32))
        tb = ctx.enter_context(nc.psum_tensor("tb", [P, 2, BANK], F32))
        ob = ctx.enter_context(nc.psum_tensor("ob", [P, OS, BANK], F32))
        raw_loaded = sem("raw_loaded")
        k_rounded, q_rounded = sem("k_rounded"), sem("q_rounded")
        head_split = sem("head_split")
        v_turned, v_ready = sem("v_turned"), sem("v_ready")
        z_ready = sem("z_ready")
        sig_done = sem("sig_done")
        masked = sem("masked")
        scanned = sem("scanned")
        w_done = sem("w_done")
        prod_set = sem("prod_set")
        w_turned = sem("w_turned")
        wt_act, wt_dve = sem("wt_act"), sem("wt_dve")
        av_done = sem("av_done")
        o_done = sem("o_done")
        head_stored = sem("head_stored")
        block = ctx.enter_context(nc.Block())

        @block.sync
        def _(sp):
            sp.sem_inc(head_stored, 16)
            stores = sb_out.rearrange("(t p) c -> p t c", p=P)

            def load(h):
                sp.wait_ge(head_split, h + 1)
                sp.nop(nofuse=True)
                sp.wait_ge(v_turned, h + 1)
                sp.nop(nofuse=True)
                for half in range(2):
                    sp.dma_start(k_raw[half * DH:(half + 1) * DH, :],
                                 projT[ds(h * DH + SK, DH), :]).then_inc(raw_loaded, 16)
                    sp.dma_start(q_raw[half * DH:(half + 1) * DH, :],
                                 projT[ds(h * DH + SQ, DH), :]).then_inc(raw_loaded, 16)
                sp.dma_start(v_raw[:, :], projT[ds(h * DH + SV, DH), :]).then_inc(raw_loaded, 16)

            def store(h):
                sp.wait_ge(o_done, h * NT + (OS + NT))
                sp.nop(nofuse=True)
                sp.dma_start(stores[:, :, ds(h * DH, DH)], head_out[:, :, :]).then_inc(head_stored, 16)

            load(0)
            with sp.Fori(0, SB_H - 1) as h:
                load(h + 1)
                store(h)
            store(SB_H - 1)
            sp.wait_ge(head_stored, SB_H * 16 + 16)

        @block.gpsimd
        def _(pool):
            with pool.Fori(0, SB_H) as h:
                pool.wait_ge(raw_loaded, h * 80 + 80)
                pool.wait_ge(z_ready, h * NP + 1)
                pool.nop(nofuse=True)
                nc.gpsimd.tensor_copy(q_both[:, :], q_raw[:, :]).then_inc(q_rounded, 1)
                for p, (i, first, end, diagonal) in enumerate(pieces):
                    if not diagonal:
                        continue
                    pool.wait_ge(sig_done, h * NP + (ZS + p + 1))
                    pool.nop(nofuse=True)
                    off = i * P - first
                    for buf, slot, fill in ((beta, p % BS, 0.0), (keep, p % SS, 1.0)):
                        part = buf[:, slot, off:off + P]
                        last = nc.gpsimd.affine_select(out=part, in_=part, compare_op=ALU.is_gt, fill=fill, base=0,
                                                       pattern=[[-1, P]], channel_multiplier=1)
                    last.then_inc(masked, 1)

        @block.scalar
        def _(act):
            act.sem_inc(sig_done, ZS)
            act.sem_inc(wt_act, 1)
            with act.Fori(0, SB_H) as h:
                act.wait_ge(raw_loaded, h * 80 + 80)
                act.wait_ge(z_ready, h * NP + 1)
                nc.scalar.activation(k_hi[:, :], k_raw[:, :], ACT.Copy).then_inc(k_rounded, 1)
                act.wait_ge(v_turned, h + 2)
                act.wait_ge(av_done, h * NG + WS)
                nc.scalar.activation(v_sb[:, 0:NT // 2, :], tb[:, 0, :].rearrange("p (k d) -> p k d", d=DH),
                                     ACT.Copy).then_inc(v_ready, 1)

                def sigmoids(p):
                    n = pieces[p][2] - pieces[p][1]
                    act.wait_ge(z_ready, h * NP + (p + 2))
                    act.wait_ge(scanned, h * NP + (p + 1))
                    before = groups_of[p - BS][-1] + 1 if p >= BS else groups_of[p - BS][-1] + 1 - NG
                    act.wait_ge(w_turned, h * NG + (NG + before))
                    nc.scalar.activation(beta[:, p % BS, 0:n], zs[:, p % ZS, 0:n], ACT.Sigmoid, scale=SCALE)
                    nc.scalar.activation(keep[:, p % SS, 0:n], zs[:, p % ZS, 0:n], ACT.Sigmoid,
                                         scale=-SCALE).then_inc(sig_done, 1)

                sigmoids(0)
                sigmoids(1)
                for p in range(NP):
                    if p + 2 < NP:
                        sigmoids(p + 2)
                    for g in groups_of[p]:
                        if g % 2 == 0:
                            n = groups[g][2] * P
                            act.wait_ge(w_turned, h * NG + (NG + g + 1))
                            act.wait_ge(av_done, h * NG + (g + 1))
                            nc.scalar.activation(wT[:, g % WS, 0:n], tb[:, 0, 0:n], ACT.Copy).then_inc(wt_act, 1)

        @block.vector
        def _(dve):
            dve.sem_inc(scanned, SS)
            dve.sem_inc(head_split, 1)
            dve.sem_inc(wt_dve, 1)
            dve.sem_inc(o_done, OS)
            nc.vector.memset(prod[:, :, :], 1.0).then_inc(prod_set, 1)
            dve.wait_ge(prod_set, 1)
            with dve.Fori(0, SB_H) as h:
                dve.wait_ge(k_rounded, h + 1)
                nc.vector.tensor_tensor(k_lo[:, :], k_raw[:, :], k_hi[:, :].bitcast(F32), ALU.subtract)
                dve.wait_ge(q_rounded, h + 1)
                nc.vector.tensor_tensor(q_both[DH:P, :], q_raw[DH:P, :], q_both[DH:P, :].bitcast(F32),
                                        ALU.subtract).then_inc(head_split, 1)
                dve.wait_ge(v_turned, h + 2)
                dve.wait_ge(av_done, h * NG + WS)
                nc.vector.tensor_copy(v_sb[:, NT // 2:NT, :],
                                      tb[:, 1, :].rearrange("p (k d) -> p k d", d=DH)).then_inc(v_ready, 1)

                def weights(p):
                    i, first, end, diagonal = pieces[p]
                    n = end - first
                    if diagonal:
                        dve.wait_ge(masked, h * NT + (i + 1))
                        initial = 1.0
                    else:
                        dve.wait_ge(sig_done, h * NP + (ZS + p + 1))
                        dve.wait_ge(scanned, h * NP + (SS + p))
                        initial = prod[:, (p - 1) % SS, 0:1]
                        nc.vector.tensor_copy(prod[:, p % SS, n:n + 1], initial)
                    s = keep[:, p % SS, 0:n][:, ::-1]
                    nc.vector.tensor_tensor_scan(prod[:, p % SS, 0:n][:, ::-1], s, s, initial,
                                                 ALU.mult, ALU.bypass).then_inc(scanned, 1)
                    dve.wait_ge(scanned, h * NP + (SS + p + 1))
                    nc.vector.tensor_tensor(beta[:, p % BS, 0:n], beta[:, p % BS, 0:n],
                                            prod[:, p % SS, 1:n + 1], ALU.mult).then_inc(w_done, 1)

                def finish(i):
                    dve.wait_ge(av_done, h * NG + (WS + last_group[i] + 1))
                    nc.vector.tensor_copy(head_out[:, i, :], ob[:, i % OS, 0:DH]).then_inc(o_done, 1)

                dve.wait_ge(head_stored, h * 16 + 16)
                weights(0)
                for p in range(NP):
                    if p + 1 < NP:
                        weights(p + 1)
                    for g in groups_of[p]:
                        if g % 2 == 1:
                            n = groups[g][2] * P
                            dve.wait_ge(w_turned, h * NG + (NG + g + 1))
                            dve.wait_ge(av_done, h * NG + (g + 1))
                            nc.vector.tensor_copy(wT[:, g % WS, 0:n], tb[:, 1, 0:n]).then_inc(wt_dve, 1)
                    if p and pieces[p - 1][1] == 0:
                        finish(pieces[p - 1][0])
                finish(NT - 1)

        @block.tensor
        def _(pe):
            pe.sem_inc(w_turned, NG)
            pe.sem_inc(v_turned, 1)
            pe.sem_inc(z_ready, 1)
            pe.sem_inc(av_done, WS)
            with pe.Fori(0, SB_H) as h:
                pe.wait_ge(raw_loaded, h * 80 + 80)
                pe.wait_ge(wt_act, h * (NG // 2) + 1)
                pe.wait_ge(wt_dve, h * (NG // 2) + 1)
                pe.nop(nofuse=True)
                for kb in range(NT):
                    last = nc.tensor.transpose(tb[:, kb // 8, kb % 8 * DH:(kb % 8 + 1) * DH],
                                               v_raw[:, kb * P:(kb + 1) * P], ident[0:DH, 0:DH])
                last.then_inc(v_turned, 1)
                pe.wait_ge(head_split, h + 2)

                def scores(p):
                    i, first, end, _ = pieces[p]
                    pe.wait_ge(sig_done, h * NP + (p + 1))
                    for c in range(first, end, BANK):
                        n = min(BANK, end - c)
                        out = zs[:, p % ZS, c - first:c - first + n]
                        nc.tensor.matmul(out, q_both[:, i * P:(i + 1) * P], k_hi[:, c:c + n], start=True, stop=False)
                        last = nc.tensor.matmul(out, q_both[:, i * P:(i + 1) * P], k_lo[:, c:c + n],
                                                start=False, stop=True)
                    last.then_inc(z_ready, 1)

                def product(g):
                    p, kb0, n = groups[g]
                    i = pieces[p][0]
                    copied = wt_act if g % 2 == 0 else wt_dve
                    pe.wait_ge(copied, h * (NG // 2) + (g // 2 + 2))
                    if g == first_group[i]:
                        pe.wait_ge(o_done, h * NT + (i + 1))
                    for j in range(n):
                        last = nc.tensor.matmul(ob[:, i % OS, 0:DH], wT[:, g % WS, j * P:(j + 1) * P],
                                                v_sb[:, kb0 + j, :], start=(g == first_group[i] and j == 0),
                                                stop=(g == last_group[i] and j == n - 1))
                    last.then_inc(av_done, 1)

                scores(0)
                scores(1)
                pe.wait_ge(v_ready, h * 2 + 2)
                for g, (p, kb0, n) in enumerate(groups):
                    if g == groups_of[p][0]:
                        if p + 2 < NP:
                            scores(p + 2)
                        pe.wait_ge(w_done, h * NP + (p + 1))
                    copied = wt_act if g % 2 == 0 else wt_dve
                    pe.wait_ge(copied, h * (NG // 2) + (g // 2 + 1))
                    first = pieces[p][1]
                    for j in range(n):
                        off = (kb0 + j) * P - first
                        last = nc.tensor.transpose(tb[:, g % 2, j * P:(j + 1) * P],
                                                   beta[:, p % BS, off:off + P], ident[:])
                    last.then_inc(w_turned, 1)
                    if g:
                        product(g - 1)
                product(NG - 1)


LEVELS = [64, 32, 16, 8, 4, 2, 1]
NL = len(LEVELS)
PAIRS = GLA_H // 2
W = PAIRS * P
MB = N_MEM // P
HW = MEM_H * DH


def prepare(nc, projT, mem, w_kv, w_alpha2, b_alpha, w_out, gsum, kmT, vm, w_hi, w_lo, level_mask, eye, ident):
    LA_C = BANK
    NLA = T // LA_C
    with ExitStack() as ctx:
        sb = lambda n, s, d=F32: ctx.enter_context(nc.sbuf_tensor(n, s, d))
        sem = lambda n: ctx.enter_context(nc.semaphore(n))
        low = sb("low", [RANK, T])
        w2 = sb("w2", [RANK, GLA_H * DK])
        b2 = sb("b2", [P, PAIRS])
        logit = sb("logit", [P, PAIRS, T])
        soft = sb("soft", [P, PAIRS, T])
        within = sb("within", [P, T])
        mem_in = sb("mem_in", [P, MB, D])
        memT = sb("memT", [P, KC, N_MEM])
        w_sb = sb("w_sb", [P, KC, 2 * HW])
        w_raw = sb("wo_raw", [P, 2, D])
        ps = ctx.enter_context(nc.psum_tensor("pre_ps", [P, 8, BANK], F32))
        low_loaded, mem_loaded, wkv_loaded = sem("low_loaded"), sem("mem_loaded"), sem("wkv_loaded")
        wo_loaded = [sem(f"wo_loaded{s}") for s in range(2)]
        wo_rounded, wo_split = sem("wo_rounded"), sem("wo_split")
        logit_ready, logit_out = sem("logit_ready"), sem("logit_out")
        soft_step, dve_step, pool_step = sem("soft_step"), sem("pre_dve"), sem("pre_pool")
        memT_ps, memT_done, kv_ps, kv_done = sem("memT_ps"), sem("memT_done"), sem("kv_ps"), sem("kv_done")
        block = ctx.enter_context(nc.Block())

        @block.sync
        def _(sp):
            sp.dma_start(low[:, :], projT[GA:GA + RANK, :]).then_inc(low_loaded, 16)
            sp.dma_start(w2[:, :], w_alpha2[0]).then_inc(low_loaded, 16)
            with nc.allow_non_contiguous_dma(reason="256 biases, once"):
                sp.dma_start(b2[:, :], b_alpha[0].rearrange("(a p) -> p a", p=P)).then_inc(low_loaded, 16)
            sp.dma_start(mem_in[:, :, :], mem[0].rearrange("(b p) d -> p b d", p=P)).then_inc(mem_loaded, 16)
            sp.dma_start(w_sb[:, :, :], w_kv[0].rearrange("(k p) c -> p k c", p=P)).then_inc(wkv_loaded, 16)
            for k in range(KC):
                if k >= 2:
                    sp.wait_ge(wo_split, k - 1)
                sp.dma_start(w_raw[:, k % 2], w_out[0, k * P:(k + 1) * P, :]).then_inc(wo_loaded[k % 2], 16)

        @block.gpsimd
        def _(pool):
            nc.gpsimd.memset(level_mask[:, :, :], 1.0).then_inc(pool_step, 1)
            pool.wait_ge(pool_step, 1)
            for l, c in enumerate(LEVELS):
                for n, (base, sign) in enumerate(((0, 1), (c - 1, -1))):
                    view = level_mask[:, l, :].rearrange("p (h b r) -> p h b r", h=GLA_H, r=c)
                    nc.gpsimd.affine_select(out=view, in_=view, compare_op=ALU.is_ge, fill=0.0, base=base,
                                            pattern=[[0, GLA_H], [-2 * c * sign, P // (2 * c)], [0, c]],
                                            channel_multiplier=sign).then_inc(pool_step, 1)
                    pool.wait_ge(pool_step, 2 + 2 * l + n)
            for k in range(KC):
                pool.wait_ge(wo_loaded[k % 2], (k // 2 + 1) * 16)
                nc.gpsimd.tensor_copy(w_hi[:, k, :], w_raw[:, k % 2, :]).then_inc(wo_rounded, 1)

        @block.tensor
        def _(pe):
            pe.wait_ge(low_loaded, 48)
            for n in range(PAIRS * NLA):
                a, c = n // NLA, n % NLA
                if n >= 2:
                    pe.wait_ge(logit_out, n - 1)
                nc.tensor.matmul(ps[:, n % 2, :], w2[:, a * P:(a + 1) * P], low[:, c * LA_C:(c + 1) * LA_C],
                                 start=True, stop=True).then_inc(logit_ready, 1)
            pe.wait_ge(mem_loaded, 16)
            for b in range(MB):
                for k in range(KC):
                    last = nc.tensor.transpose(ps[:, 2 + 2 * b + k // 4, k % 4 * P:(k % 4 + 1) * P],
                                               mem_in[:, b, k * P:(k + 1) * P], ident[:])
                last.then_inc(memT_ps, 1)
            pe.wait_ge(memT_done, MB)
            pe.wait_ge(wkv_loaded, 16)
            for a in range(2):
                for k in range(KC):
                    nc.tensor.matmul(ps[:, 6 + a, 0:N_MEM], w_sb[:, k, a * P:(a + 1) * P], memT[:, k, :],
                                     start=(k == 0), stop=(k == KC - 1))
            for b in range(MB):
                for k in range(KC):
                    last = nc.tensor.matmul(ps[:, 2 + b, 0:HW], memT[:, k, b * P:(b + 1) * P], w_sb[:, k, HW:2 * HW],
                                            start=(k == 0), stop=(k == KC - 1))
            last.then_inc(kv_ps, 1)

        @block.scalar
        def _(act):
            for n in range(PAIRS * NLA):
                a, c = n // NLA, n % NLA
                cols = slice(c * LA_C, (c + 1) * LA_C)
                act.wait_ge(logit_ready, n + 1)
                nc.scalar.activation(logit[:, a, cols], ps[:, n % 2, :], ACT.Identity, bias=b2[:, a:a + 1])
                nc.scalar.activation(soft[:, a, cols], ps[:, n % 2, :], ACT.Abs, bias=b2[:, a:a + 1]).then_inc(logit_out, 1)
            act.wait_ge(logit_out, PAIRS * NLA)
            nc.scalar.activation(soft[:, :, :], soft[:, :, :], ACT.Exp, scale=-1.0).then_inc(soft_step, 1)
            act.wait_ge(soft_step, 1)
            nc.scalar.activation(soft[:, :, :], soft[:, :, :], ACT.Ln, bias=1.0).then_inc(soft_step, 1)
            act.wait_ge(memT_ps, 1)
            nc.scalar.activation(memT[:, :, 0:P], ps[:, 2:4, :].rearrange("p b (k t) -> p (b k) t", t=P),
                                 ACT.Copy).then_inc(memT_done, 1)
            act.wait_ge(kv_ps, 1)
            nc.scalar.activation(kmT[:, :, :], ps[:, 6:8, 0:N_MEM], ACT.Copy).then_inc(kv_done, 1)

        @block.vector
        def _(dve):
            nc.vector.memset(within[:, :], 1.0).then_inc(dve_step, 1)
            for h in range(GLA_H):
                nc.vector.tensor_copy(eye[:, h * P:(h + 1) * P], ident[:, :])
            dve.wait_ge(dve_step, 1)
            nc.vector.memset(within[:, :].rearrange("p (n c) -> p n c", c=P)[:, :, 0:1], 0.0).then_inc(dve_step, 1)
            dve.wait_ge(memT_ps, 2)
            nc.vector.tensor_copy(memT[:, :, P:2 * P], ps[:, 4:6, :].rearrange("p b (k t) -> p (b k) t", t=P)
                                  ).then_inc(memT_done, 1)
            dve.wait_ge(soft_step, 2)
            nc.vector.scalar_tensor_tensor(soft[:, :, :], logit[:, :, :], 0.0, soft[:, :, :], ALU.min,
                                           ALU.subtract).then_inc(dve_step, 1)
            for k in range(KC):
                dve.wait_ge(wo_rounded, k + 1)
                nc.vector.tensor_tensor(w_lo[:, k, :], w_raw[:, k % 2, :], w_hi[:, k, :].bitcast(F32),
                                        ALU.subtract).then_inc(wo_split, 1)
            dve.wait_ge(dve_step, 3)
            for a in range(PAIRS):
                nc.vector.tensor_tensor_scan(gsum[:, a, :], within[:, :], soft[:, a, :], 0.0, ALU.mult, ALU.add)
            dve.wait_ge(kv_ps, 1)
            nc.vector.tensor_copy(vm[:, :, :], ps[:, 2:4, 0:HW]).then_inc(kv_done, 1)


def done(n, back=0):
    return n + (3 - back)


def mix_and_project(nc, x, sb_out, projT, gla_nw, ln_g, ln_b, gsum, kmT, vm, w_hi, w_lo, level_mask, eye, ident, out):
    TO_END, FROM_START, NF = NL, NL + 1, NL + 2
    LAST = NT - 1
    SLICES = ((0, 0, 16), (0, 16, 24), (1, 0, 8), (1, 8, 16), (1, 16, 24))
    with ExitStack() as ctx:
        sb = lambda n, s, d=F32: ctx.enter_context(nc.sbuf_tensor(n, s, d))
        sems = []

        def sem(name):
            sems.append(ctx.enter_context(nc.semaphore(name)))
            return sems[-1]

        qk = sb("qk", [P, 2, 2 * W])
        vT = sb("vT", [P, GLA_H, P])
        v_sb = sb("gv_sb", [P, GLA_H * DV])
        fac = sb("fac", [P, NF, W])
        m = sb("m", [P, 2, NF, W])
        end_decay = sb("end_decay", [P, 2, PAIRS])
        kd = sb("kd", [P, W])
        att = sb("att", [P, GLA_H, P])
        state = sb("state", [P, 2, PAIRS, DV])
        squares = sb("squares", [P, GLA_H, DV])
        square_sum = sb("square_sum", [P, GLA_H])
        rms = sb("rms", [P, GLA_H])
        newton = sb("newton", [P, 2, 2 * GLA_H])
        mq = sb("mq", [P, 2, P])
        top = sb("top", [P, MEM_H])
        probs = sb("probs", [P, MEM_H, N_MEM])
        total = sb("total", [P, MEM_H])
        inverse = sb("inverse", [P, MEM_H])
        probsT = sb("probsT", [P, MEM_H * MB, P])
        mixed = sb("mixed", [P, D])
        nw = sb("nw", [P, 1])
        ln_w = sb("ln_w", [P, D])
        ln_c = sb("ln_c", [P, D])
        eps = sb("eps", [P, 2])
        gate = sb("gate", [P, KC, P])
        x_sb = sb("x_sb", [P, D])
        gated = sb("gated", [P, KC, P])
        g_hi = sb("g_hi", [P, KC, P], F32R)
        g_lo = sb("g_lo", [P, KC, P], F32R)
        y = sb("y", [P, 2, D])
        stats = sb("stats", [P, 2, 2, 6])
        mean_var = sb("mean_var", [P, 2, 2])
        rstd = sb("rstd", [P, 2])
        bank = ctx.enter_context(nc.psum_tensor("bank", [P, 8, BANK], F32))
        st_ps = bank[:, 3, W:2 * W]
        kd_ps = bank[:, 4, 0:W]
        o_ps = bank[:, 4, :]
        v_ps = bank[:, 5, :]
        mo_ps = bank[:, 5, 0:HW]
        Y0 = 6

        consts_set, consts_loaded = sem("consts_set"), sem("consts_loaded")
        sems.clear()
        qk_loaded = [ctx.enter_context(nc.semaphore(f"qk_loaded{s}")) for s in range(2)]
        vT_loaded, mq_loaded, gate_loaded, x_loaded, sb_loaded = (
            ctx.enter_context(nc.semaphore(n)) for n in ("vT_loaded", "mq_loaded", "gate_loaded", "xr_loaded", "sb_loaded"))
        out_stored = [ctx.enter_context(nc.semaphore(f"out_stored{s}")) for s in range(2)]
        diffs = sem("diffs")
        weighted = sem("weighted")
        pool_sems, sems[:] = list(sems), []
        g_copied, abs_done, fac_done = sem("g_copied"), sem("abs_done"), sem("fac_done")
        natural = sem("natural")
        squared, mean_ln, rms_done = sem("squared"), sem("mean_ln"), sem("rms_done")
        exp_done, pt_act, hi_done = sem("exp_done"), sem("pt_act"), sem("hi_done")
        var_ln, rstd_done = sem("var_ln"), sem("rstd_done")
        act_sems, sems[:] = list(sems), []
        m_done, st_done, max_done, top_done = sem("m_done"), sem("st_done"), sem("max_done"), sem("top_done")
        lev_read = [sem(f"lev_read{b}") for b in range(5)]
        o_read = sem("o_read")
        pt_dve, inv_done, mo_read = sem("pt_dve"), sem("inv_done"), sem("mo_read")
        gated_done, lo_done = sem("gated_done"), sem("lo_done")
        y_read = [sem(f"y_read{c}") for c in range(2)]
        stats_done, aggregated, scaled, final = sem("stats_done"), sem("aggregated"), sem("scaled"), sem("final")
        dve_sems, sems[:] = list(sems), []
        overlaid = ctx.enter_context(nc.semaphore("overlaid"))
        refined = [ctx.enter_context(nc.semaphore(n)) for n in ("rms_refined", "dev_refined")]
        turned = sem("turned")
        even_done = [sem(f"even_done{b}") for b in range(5)]
        lev_ready = [sem(f"lev_ready{b}") for b in range(5)]
        o_even, o_ready, st_ready, s_ready = sem("o_even"), sem("o_ready"), sem("st_ready"), sem("s_ready")
        pt_ready, mo_ready, mt_ready = sem("pt_ready"), sem("mo_ready"), sem("mt_ready")
        y_ready = [sem(f"y_ready{c}") for c in range(2)]
        pe_sems = list(sems)
        block = ctx.enter_context(nc.Block())

        def place(h):
            return h % 2 * 2 + h // 2

        def head_rows(h):
            return slice(h % 2 * DK, h % 2 * DK + DK)

        def blocks(ap, c):
            return ap.rearrange("p (n h c) -> p n h c", h=2, c=c)

        def roles(s, c):
            v = qk[:, s, :]
            return bass.AP(v.tensor, v.offset, [list(v.ap[0]), [2 * c, W // (2 * c)], [W + c, 2], [1, c]])

        @block.sync
        def _(sp):
            with nc.allow_non_contiguous_dma(reason="128 weights, once"):
                sp.dma_start(nw[:, :], gla_nw[0].rearrange("(p a) -> p a", a=1)).then_inc(consts_loaded, 16)
            sp.dma_start(ln_w[:, :], ln_g[0].partition_broadcast(P)).then_inc(consts_loaded, 16)
            sp.dma_start(ln_c[:, :], ln_b[0].partition_broadcast(P)).then_inc(consts_loaded, 16)
            for s in range(2):
                sp.sem_inc(out_stored[s], 16)

            def cols(row, n, t):
                return projT[row:row + n * P, ds(t * P, P)].rearrange("(c p) t -> p c t", p=P)

            def load_qk(t, s):
                sp.wait_ge(m_done, done(t, 2))
                sp.nop(nofuse=True)
                sp.wait_ge(lev_ready[4], done(t, 2))
                sp.nop(nofuse=True)
                for at, row in ((0, GK), (W, GQ)):
                    sp.dma_start(qk[:, s, at:at + W].rearrange("p (a t) -> p a t", t=P), cols(row, PAIRS, t)
                                 ).then_inc(qk_loaded[s], 16)

            load_qk(0, 0)

            def load_x(t, back):
                sp.wait_ge(y_read[0], done(t, back + 1))
                sp.nop(nofuse=True)
                sp.wait_ge(y_read[1], done(t, back + 1))
                sp.nop(nofuse=True)
                sp.dma_start(x_sb[:, :], x[0, ds((t - back) * P if isinstance(t, int) else t * P - back * P, P), :]
                             ).then_inc(x_loaded, 16)

            def step(t, s, y1=True):
                sp.wait_ge(turned, done(t, 1))
                sp.nop(nofuse=True)
                sp.dma_start(vT[:, :, :], cols(GV, GLA_H, t)).then_inc(vT_loaded, 16)
                if not (isinstance(t, int) and t == LAST):
                    load_qk(t + 1, 1 - s)
                sp.wait_ge(s_ready, done(t, 1))
                sp.nop(nofuse=True)
                sp.dma_start(mq[:, :, :], cols(MQ, 2, t)).then_inc(mq_loaded, 16)
                sp.wait_ge(mt_ready, done(t, 1))
                sp.nop(nofuse=True)
                sp.dma_start(mixed[:, MIX_SB:MIX_MEM], sb_out[ds(t * P, P), :]).then_inc(sb_loaded, 16)
                if y1:
                    load_x(t, 1)
                sp.wait_ge(gated_done, done(t, 1))
                sp.nop(nofuse=True)
                for c0, cn, row in ((0, 4, GG), (4, 2, SG), (6, 2, MG)):
                    sp.dma_start(gate[:, c0:c0 + cn], cols(row, cn, t)).then_inc(gate_loaded, 16)

            step(0, 0, y1=False)
            with sp.Fori(0, (NT - 2) // 2) as it:
                step(it * 2 + 1, 1)
                step(it * 2 + 2, 0)
            step(LAST, 1)
            load_x(LAST, 0)

        @block.gpsimd
        def _(pool):
            for s in pool_sems:
                pool.sem_inc(s, 2)
            nc.gpsimd.memset(att[:, :, :], 0.0).then_inc(consts_set, 1)
            nc.gpsimd.memset(state[:, 0], 0.0).then_inc(consts_set, 1)

            def differences(t):
                pool.wait_ge(g_copied, done(t))
                pool.nop(nofuse=True)
                g = fac[:, FROM_START, :]
                for l, c in enumerate(LEVELS):
                    gm = blocks(g, c)[:, :, 0:1, c - 1:c].rearrange("p n a b -> p n (a b)")
                    view = lambda ap: ap.rearrange("p (n c) -> p n c", c=2 * c)
                    nc.gpsimd.tensor_tensor(view(fac[:, l, :]), view(g),
                                            gm.to_broadcast([P, W // (2 * c), 2 * c]), ALU.subtract)
                view = lambda ap: ap.rearrange("p (n c) -> p n c", c=P)
                nc.gpsimd.tensor_tensor(view(fac[:, TO_END, :]), view(g),
                                        view(g)[:, :, P - 1:P].to_broadcast([P, PAIRS, P]),
                                        ALU.subtract).then_inc(diffs, 1)

            def weigh(t, s, back):
                pool.wait_ge(scaled, done(t, back))
                pool.nop(nofuse=True)
                nc.gpsimd.tensor_tensor(y[:, s, :], y[:, s, :], ln_w[:, :], ALU.mult).then_inc(weighted, 1)

            differences(0)
            pool.wait_ge(consts_loaded, 48)

            def step(t, s):
                if not (isinstance(t, int) and t == LAST):
                    differences(t + 1)
                weigh(t, s, 2)

            differences(1)
            differences(2)
            with pool.Fori(0, (NT - 4) // 2) as it:
                step(it * 2 + 2, 0)
                step(it * 2 + 3, 1)
            step(LAST - 1, 0)
            step(LAST, 1)
            for t in (LAST - 1, LAST):
                weigh(t, t % 2, 0)

        @block.scalar
        def _(act):
            nc.scalar.add_instruction(mybir.InstLoadActFuncSet(name=nc.get_next_instruction_name(), ins=[], outs=[], act_func_set_id=6))
            for s in act_sems:
                act.sem_inc(s, 2)

            def copy_g(t):
                act.wait_ge(m_done, done(t, 1))
                act.wait_ge(fac_done, done(t, 1))
                nc.scalar.activation(fac[:, FROM_START, :].rearrange("p (a t) -> p a t", t=P),
                                     gsum[:, :, ds(t * P, P)], ACT.Copy, scale=1.0 / 16.0).then_inc(g_copied, 1)

            def factors(t, s):
                act.wait_ge(diffs, done(t))
                nc.scalar.activation(fac[:, :, :], fac[:, :, :], ACT.Abs).then_inc(abs_done, 1)
                act.wait_ge(abs_done, done(t))
                nc.scalar.activation(fac[:, :, :], fac[:, :, :], ACT.Exp, scale=-1.0).then_inc(fac_done, 1)

            def take_natural(t):
                act.wait_ge(turned, done(t))
                act.wait_ge(st_ready, done(t, 1))
                nc.scalar.activation(v_sb[:, :], v_ps, ACT.Copy)
                nc.scalar.activation(kd[:, :], kd_ps, ACT.Copy).then_inc(natural, 1)

            def root_mean_square(t):
                act.wait_ge(o_ready, done(t))
                act.wait_ge(o_read, done(t, 1))
                act.wait_ge(squared, done(t, 1))
                for h in range(GLA_H):
                    last = nc.scalar.activation(squares[:, h, :], o_ps[:, h * DV:(h + 1) * DV], ACT.Square,
                                                scale=SCALE, accum_out=square_sum[:, h:h + 1])
                last.then_inc(squared, 1)
                act.wait_ge(squared, done(t))
                nc.scalar.activation(rms[:, :], square_sum[:, :], ACT.Ln, bias=eps[:, 0:1], scale=1.0 / DV).then_inc(mean_ln, 1)
                act.wait_ge(mean_ln, done(t))
                nc.scalar.activation(rms[:, :], rms[:, :], ACT.Exp, scale=-0.5).then_inc(rms_done, 1)

            def exps(t):
                act.wait_ge(top_done, done(t))
                act.wait_ge(pt_ready, done(t, 1))
                act.wait_ge(mo_read, done(t, 1))
                for h in range(MEM_H):
                    j = place(h)
                    last = nc.scalar.activation(probs[:, h, :], bank[:, j // 2, j % 2 * N_MEM:(j % 2 + 1) * N_MEM], ACT.Exp,
                                                bias=top[:, j:j + 1], scale=SCALE, accum_out=total[:, h:h + 1])
                last.then_inc(exp_done, 1)

            def copy_probs(t):
                act.wait_ge(pt_ready, done(t))
                act.wait_ge(mo_ready, done(t, 1))
                nc.scalar.activation(probsT[:, 0:4, :], bank[:, 2, :].rearrange("p (j t) -> p j t", t=P),
                                     ACT.Copy).then_inc(pt_act, 1)

            def round_gated(t, back):
                act.wait_ge(gated_done, done(t, back))
                act.wait_ge(y_ready[1], done(t, back + 1))
                nc.scalar.activation(g_hi[:, :, :], gated[:, :, :], ACT.Copy).then_inc(hi_done, 1)

            def deviation(t, s, back):
                act.wait_ge(aggregated, done(t, back))
                nc.scalar.activation(rstd[:, s:s + 1], mean_var[:, s, 1:2], ACT.Ln, bias=eps[:, 1:2]).then_inc(var_ln, 1)
                act.wait_ge(var_ln, done(t, back))
                nc.scalar.activation(rstd[:, s:s + 1], rstd[:, s:s + 1], ACT.Exp, scale=-0.5).then_inc(rstd_done, 1)

            def store(t, s, back):
                act.wait_ge(final, done(t, back))
                act.dma_start(out[0, ds((t - back) * P if isinstance(t, int) else t * P - back * P, P), :],
                              y[:, s, :]).then_inc(out_stored[s], 16)

            copy_g(0)
            factors(0, 0)
            act.wait_ge(consts_set, 4)

            def step(t, s, y1=True, y2=True):
                take_natural(t)
                if not (isinstance(t, int) and t == LAST):
                    copy_g(t + 1)
                if y1:
                    round_gated(t, 1)
                if y2:
                    deviation(t, s, 2)
                if not (isinstance(t, int) and t == LAST):
                    factors(t + 1, 1 - s)
                root_mean_square(t)
                exps(t)
                copy_probs(t)
                if y2:
                    store(t, s, 2)

            step(0, 0, y1=False, y2=False)
            step(1, 1, y2=False)
            with act.Fori(0, (NT - 4) // 2) as it:
                step(it * 2 + 2, 0)
                step(it * 2 + 3, 1)
            step(LAST - 1, 0)
            step(LAST, 1)
            round_gated(LAST, 0)
            for t in (LAST - 1, LAST):
                deviation(t, t % 2, 0)
                store(t, t % 2, 0)
            for s in range(2):
                act.wait_ge(out_stored[s], 16 * (NT // 2 + 1))

        @block.vector
        def _(dve):
            for s in dve_sems:
                dve.sem_inc(s, 2)
            dve.sem_inc(overlaid, NL + 1)
            for r in refined:
                dve.sem_inc(r, 8)
            nc.vector.memset(eps[:, 0:1], RMS_EPS).then_inc(consts_set, 1)
            nc.vector.memset(eps[:, 1:2], LN_EPS).then_inc(consts_set, 1)

            def multiply(t, s):
                dve.wait_ge(fac_done, done(t))
                dve.wait_ge(qk_loaded[s], (t - s) * 16 + 32)
                dve.wait_ge(o_ready, done(t, 2))
                for l, c in enumerate(LEVELS):
                    nc.vector.tensor_tensor(blocks(m[:, s, l, :], c), roles(s, c), blocks(fac[:, l, :], c), ALU.mult)
                nc.vector.tensor_tensor(m[:, s, TO_END, :], qk[:, s, 0:W], fac[:, TO_END, :], ALU.mult)
                dve.wait_ge(st_done, done(t, 2))
                nc.vector.tensor_copy(end_decay[:, s, :], fac[:, FROM_START, :].rearrange(
                    "p (a t) -> p a t", t=P)[:, :, P - 1:P].rearrange("p a b -> p (a b)"))
                nc.vector.tensor_tensor(m[:, s, FROM_START, :], qk[:, s, W:2 * W], fac[:, FROM_START, :],
                                        ALU.mult).then_inc(m_done, 1)

            n_overlay = {l: n for n, l in enumerate((4, 5, 6, 0, 1, 2, 3, NL))}

            def overlay(t, b):
                for l in (range(2 * b, min(2 * b + 2, NL)) if b < 4 else (NL,)):
                    dve.wait_ge(lev_ready[b], done(t))
                    dve.wait_ge(overlaid, t * (NL + 1) + (NL + 1 + n_overlay[l]))
                    if l == 4:
                        dve.wait_ge(o_ready, done(t, 1))
                    dve.nop(nofuse=True)
                    if l == NL:
                        ins = nc.vector.copy_predicated(att[:, :, :], eye[:, :].bitcast(I32).rearrange("p (h t) -> p h t", t=P),
                                                        bank[:, 4, :].rearrange("p (h t) -> p h t", t=P))
                    else:
                        c = LEVELS[l]
                        out_ = att[:, :, :].rearrange("p h (b u r) -> p h b u r", u=2, r=c)[:, :, :, 1, :]
                        shape = "p (h b r) -> p h b r"
                        ins = nc.vector.copy_predicated(
                            out_, level_mask[:, l, :].bitcast(I32).rearrange(shape, h=GLA_H, r=c),
                            bank[:, b, (l % 2) * W:(l % 2 + 1) * W].rearrange(shape, h=GLA_H, r=c))
                    ins.then_inc(overlaid, 1)
                dve.wait_ge(overlaid, t * (NL + 1) + (NL + 1 + n_overlay[l] + 1))
                dve.sem_inc(lev_read[b], 1)

            def update_state(t, s):
                dve.wait_ge(st_ready, done(t))
                for a in range(PAIRS):
                    last = nc.vector.scalar_tensor_tensor(state[:, 1 - s, a, :], state[:, s, a, :], end_decay[:, s, a:a + 1],
                                                          st_ps[:, a * DV:(a + 1) * DV], ALU.mult, ALU.add)
                last.then_inc(st_done, 1)

            def refine(n, t, back, root, value, scale, addend):
                width = root.shape[-1]
                v, a = newton[:, n, 0:width], newton[:, n, GLA_H:GLA_H + width]
                at = t * 4 + (8 - 4 * back)
                nc.vector.tensor_scalar(v, value, scale, addend, ALU.mult, ALU.add).then_inc(refined[n], 1)
                nc.vector.scalar_tensor_tensor(a, root, -0.5, root, ALU.mult, ALU.mult).then_inc(refined[n], 1)
                dve.wait_ge(refined[n], at + 2)
                nc.vector.tensor_tensor(a, a, v, ALU.mult).then_inc(refined[n], 1)
                dve.wait_ge(refined[n], at + 3)
                nc.vector.scalar_tensor_tensor(root, a, 1.5, root, ALU.add, ALU.mult).then_inc(refined[n], 1)
                dve.wait_ge(refined[n], at + 4)

            def take_gla(t):
                dve.wait_ge(rms_done, done(t))
                refine(0, t, 0, rms[:, :], square_sum[:, :], 1.0 / DV, RMS_EPS)
                dve.wait_ge(mt_ready, done(t, 1))
                nc.vector.scalar_tensor_tensor(
                    mixed[:, 0:GLA_H * DV].rearrange("p (h d) -> p h d", d=DV), o_ps.rearrange("p (h d) -> p h d", d=DV),
                    SCALE, rms[:, :].rearrange("p (h a) -> p h a", a=1).to_broadcast([P, GLA_H, DV]),
                    ALU.mult, ALU.mult).then_inc(o_read, 1)

            def maxima(t):
                dve.wait_ge(s_ready, done(t))
                dve.wait_ge(exp_done, done(t, 1))
                nc.vector.reduce_max(top[:, :], bank[:, 0:2, :].rearrange("p b (h m) -> p (b h) m", m=N_MEM),
                                     AX.X).then_inc(max_done, 1)
                dve.wait_ge(max_done, done(t))
                nc.vector.tensor_scalar(top[:, :], top[:, :], -SCALE, None, ALU.mult).then_inc(top_done, 1)

            def copy_probs(t):
                dve.wait_ge(pt_ready, done(t))
                dve.wait_ge(mo_ready, done(t, 1))
                nc.vector.tensor_copy(probsT[:, 4:8, :], bank[:, 3, :].rearrange("p (j t) -> p j t", t=P)
                                      ).then_inc(pt_dve, 1)
                nc.vector.reciprocal(inverse[:, :], total[:, :]).then_inc(inv_done, 1)

            def take_memory(t):
                dve.wait_ge(inv_done, done(t))
                dve.wait_ge(mo_ready, done(t))
                nc.vector.tensor_tensor(mixed[:, MIX_MEM:MIX_MEM + HW].rearrange("p (h d) -> p h d", d=DH),
                                        mo_ps.rearrange("p (h d) -> p h d", d=DH),
                                        inverse[:, :].rearrange("p (h a) -> p h a", a=1).to_broadcast([P, MEM_H, DH]),
                                        ALU.mult).then_inc(mo_read, 1)

            def gating(t, back):
                dve.wait_ge(mt_ready, done(t, back))
                dve.wait_ge(gate_loaded, t * 48 + 48 * (1 - back))
                dve.wait_ge(lo_done, done(t, back + 1))
                parts = bank[:, 0:2, :].rearrange("p b (c t) -> p (b c) t", t=P)
                nc.vector.scalar_tensor_tensor(gated[:, 0:GLA_H, :], parts[:, 0:GLA_H, :], nw[:, 0:1],
                                               gate[:, 0:GLA_H, :], ALU.mult, ALU.mult)
                nc.vector.tensor_tensor(gated[:, GLA_H:KC, :], parts[:, GLA_H:KC, :], gate[:, GLA_H:KC, :],
                                        ALU.mult).then_inc(gated_done, 1)

            def lower_part(t, back):
                dve.wait_ge(hi_done, done(t, back))
                nc.vector.tensor_tensor(g_lo[:, :, :], gated[:, :, :], g_hi[:, :, :].bitcast(F32),
                                        ALU.subtract).then_inc(lo_done, 1)

            def residual(t, s, c, back):
                dve.wait_ge(y_ready[c], done(t, back))
                if c == 0:
                    dve.wait_ge(x_loaded, t * 16 + 16 * (1 - back))
                    dve.wait_ge(out_stored[s], (t - back - s) * 8 + 16 if isinstance(t, int) else (t + (-back - s)) * 8 + 16)
                cols = slice(c * BANK, (c + 1) * BANK)
                nc.vector.scalar_tensor_tensor(y[:, s, cols], x_sb[:, cols], ALPHA, bank[:, Y0 + c, :],
                                               ALU.mult, ALU.add).then_inc(y_read[c], 1)

            def statistics(t, s, back):
                dve.wait_ge(y_read[1], done(t, back))
                for c in range(2):
                    last = nc.vector.bn_stats(stats[:, s, c, :], y[:, s, c * BANK:(c + 1) * BANK])
                last.then_inc(stats_done, 1)
                dve.wait_ge(stats_done, done(t, back))
                dve.nop(nofuse=True)
                nc.vector.bn_aggr(mean_var[:, s, :], stats[:, s].rearrange("p c k -> p (c k)")).then_inc(aggregated, 1)

            def normalise(t, s, back):
                dve.wait_ge(rstd_done, done(t, back))
                refine(1, t, back, rstd[:, s:s + 1], mean_var[:, s, 1:2], 1.0, LN_EPS)
                nc.vector.tensor_scalar(y[:, s, :], y[:, s, :], mean_var[:, s, 0:1], rstd[:, s:s + 1],
                                        ALU.subtract, ALU.mult).then_inc(scaled, 1)

            def shift(t, s, back):
                dve.wait_ge(weighted, done(t, back))
                nc.vector.tensor_tensor(y[:, s, :], y[:, s, :], ln_c[:, :], ALU.add).then_inc(final, 1)

            multiply(0, 0)
            dve.wait_ge(consts_set, 4)
            dve.wait_ge(consts_loaded, 48)

            def step(t, s, y1=True, y2=True):
                if y1:
                    gating(t, 1)
                for b in (2, 3):
                    overlay(t, b)
                if y1:
                    lower_part(t, 1)
                if y2:
                    residual(t, s, 1, 2)
                    statistics(t, s, 2)
                for b in (0, 1, 4):
                    overlay(t, b)
                if y2:
                    normalise(t, s, 2)
                update_state(t, s)
                maxima(t)
                if y1:
                    residual(t, 1 - s, 0, 1)
                if not (isinstance(t, int) and t == LAST):
                    multiply(t + 1, 1 - s)
                if y2:
                    shift(t, s, 2)
                take_gla(t)
                copy_probs(t)
                take_memory(t)

            step(0, 0, y1=False, y2=False)
            step(1, 1, y2=False)
            with dve.Fori(0, (NT - 4) // 2) as it:
                step(it * 2 + 2, 0)
                step(it * 2 + 3, 1)
            step(LAST - 1, 0)
            step(LAST, 1)
            gating(LAST, 0)
            lower_part(LAST, 0)
            residual(LAST - 1, 0, 1, 0)
            statistics(LAST - 1, 0, 0)
            normalise(LAST - 1, 0, 0)
            shift(LAST - 1, 0, 0)
            for c in range(2):
                residual(LAST, 1, c, 0)
            statistics(LAST, 1, 0)
            normalise(LAST, 1, 0)
            shift(LAST, 1, 0)

        @block.tensor
        def _(pe):
            for s in pe_sems:
                pe.sem_inc(s, 2)

            def turn_inputs(t, s):
                pe.wait_ge(vT_loaded, t * 16 + 16)
                pe.wait_ge(m_done, done(t))
                pe.wait_ge(mo_read, done(t, 1))
                pe.wait_ge(o_read, done(t, 1))
                pe.nop(nofuse=True)
                for h in range(GLA_H):
                    nc.tensor.transpose(v_ps[:, h * DV:(h + 1) * DV], vT[:, h, :], ident[:])
                for a in range(PAIRS):
                    last = nc.tensor.transpose(kd_ps[:, a * P:(a + 1) * P], m[:, s, TO_END, a * P:(a + 1) * P], ident[:])
                last.then_inc(turned, 1)

            def turn_mixed(t, back):
                pe.wait_ge(o_read, done(t, back))
                pe.wait_ge(mo_read, done(t, back))
                pe.wait_ge(sb_loaded, t * 16 + 16 * (1 - back))
                pe.nop(nofuse=True)
                for c in range(KC):
                    last = nc.tensor.transpose(bank[:, c // 4, c % 4 * P:(c % 4 + 1) * P], mixed[:, c * P:(c + 1) * P], ident[:])
                last.then_inc(mt_ready, 1)

            def levels(t, s, y1):
                for group in ((2, 3), (0, 1), (4,)):
                    for odd in range(2):
                        for b in group:
                            if odd:
                                pe.wait_ge(even_done[b], done(t))
                            elif b in (2, 3):
                                pe.wait_ge(pt_act if b == 2 else pt_dve, done(t, 1))
                            elif b in (0, 1):
                                pe.wait_ge(gated_done if y1 else exp_done, done(t, 1))
                            else:
                                pe.wait_ge(natural, done(t))
                            for l in (range(2 * b, min(2 * b + 2, NL)) if b < 4 else (NL,)):
                                for h in range(odd, GLA_H, 2):
                                    rows, a = head_rows(h), h // 2
                                    if l == NL:
                                        last = nc.tensor.matmul(bank[:, 4, h * P:(h + 1) * P], qk[rows, s, a * P:(a + 1) * P],
                                                                qk[rows, s, W + a * P:W + (a + 1) * P], start=True, stop=True)
                                        continue
                                    c = LEVELS[l]
                                    mine = m[rows, s, l, a * P:(a + 1) * P]
                                    at = (l % 2) * W + h * (P // 2)
                                    last = nc.tensor.matmul(bank[:, b, at:at + P // 2].rearrange("p (b r) -> p b r", r=c), mine,
                                                            mine.rearrange("p (b u r) -> p b u r", u=2, r=c)[:, :, 1, :],
                                                            start=True, stop=True)
                            last.then_inc(lev_ready[b] if odd else even_done[b], 1)

            def attend(t, s):
                for b in (4, 0, 1, 2, 3):
                    pe.wait_ge(lev_read[b], done(t))
                pe.wait_ge(st_done, done(t, 1))
                for h in (0, 2, 1, 3):
                    rows, a = head_rows(h), h // 2
                    if h == 1:
                        pe.wait_ge(o_even, done(t))
                    nc.tensor.matmul(o_ps[:, h * DV:(h + 1) * DV], m[rows, s, FROM_START, a * P:(a + 1) * P],
                                     state[rows, s, a, :], start=True, stop=False)
                    last = nc.tensor.matmul(o_ps[:, h * DV:(h + 1) * DV], att[:, h, :], v_sb[:, h * DV:(h + 1) * DV],
                                            start=False, stop=True)
                    if h == 2:
                        last.then_inc(o_even, 1)
                last.then_inc(o_ready, 1)
                for h in range(GLA_H):
                    at = h // 2 * P + h % 2 * DK
                    last = nc.tensor.matmul(st_ps[head_rows(h), h // 2 * DV:(h // 2 + 1) * DV], kd[:, at:at + DK],
                                            v_sb[:, h * DV:(h + 1) * DV], start=True, stop=True)
                last.then_inc(st_ready, 1)

            def memory_scores(t):
                pe.wait_ge(mq_loaded, t * 16 + 16)
                for h in range(MEM_H):
                    j = place(h)
                    last = nc.tensor.matmul(bank[:, j // 2, j % 2 * N_MEM:(j % 2 + 1) * N_MEM], mq[head_rows(h), h // 2, :],
                                            kmT[head_rows(h), h // 2, :], start=True, stop=True)
                last.then_inc(s_ready, 1)

            def turn_probs(t):
                pe.wait_ge(exp_done, done(t))
                pe.wait_ge(st_done, done(t))
                pe.nop(nofuse=True)
                for j in range(MEM_H * MB):
                    last = nc.tensor.transpose(bank[:, 2 + j // 4, j % 4 * P:(j % 4 + 1) * P],
                                               probs[:, j // MB, j % MB * P:(j % MB + 1) * P], ident[:])
                last.then_inc(pt_ready, 1)

            def memory_output(t):
                pe.wait_ge(pt_act, done(t))
                pe.wait_ge(pt_dve, done(t))
                for j in range(MEM_H * MB):
                    h, b = j // MB, j % MB
                    last = nc.tensor.matmul(mo_ps[:, h * DH:(h + 1) * DH], probsT[:, j, :], vm[:, b, h * DH:(h + 1) * DH],
                                            start=(b == 0), stop=(b == MB - 1))
                last.then_inc(mo_ready, 1)

            def project_slice(t, n, back):
                c, first, end = SLICES[n]
                if n == 0:
                    pe.wait_ge(lo_done, done(t, back))
                if first == 0:
                    pe.wait_ge(y_read[c], done(t, back + 1))
                for i in range(first, end):
                    k, (g, w) = i // 3, ((g_hi, w_hi), (g_hi, w_lo), (g_lo, w_hi))[i % 3]
                    last = nc.tensor.matmul(bank[:, Y0 + c, :], g[:, k, :], w[:, k, c * BANK:(c + 1) * BANK],
                                            start=(i == 0), stop=(i == 3 * KC - 1))
                if end == 3 * KC:
                    last.then_inc(y_ready[c], 1)

            def step(t, s, y1=True):
                turn_inputs(t, s)
                if y1:
                    turn_mixed(t, 1)
                levels(t, s, y1)
                if y1:
                    project_slice(t, 0, 1)
                attend(t, s)
                memory_scores(t)
                if y1:
                    project_slice(t, 1, 1)
                    project_slice(t, 2, 1)
                turn_probs(t)
                if y1:
                    project_slice(t, 3, 1)
                memory_output(t)
                if y1:
                    project_slice(t, 4, 1)

            pe.wait_ge(consts_set, 4)
            step(0, 0, y1=False)
            with pe.Fori(0, (NT - 2) // 2) as it:
                step(it * 2 + 1, 1)
                step(it * 2 + 2, 0)
            step(LAST, 1)
            turn_mixed(LAST, 0)
            for n in range(len(SLICES)):
                project_slice(LAST, n, 0)


def last_stage(nc, x, mem, w_alpha2, b_alpha, gla_norm_w, w_mem_kv, w_out, ln_g, ln_b, sb_out, projT, ident, out):
    with ExitStack() as ctx:
        sb = lambda n, s, d=F32: ctx.enter_context(nc.sbuf_tensor(n, s, d))
        gsum = sb("gsum", [P, PAIRS, T])
        kmT = sb("kmT", [P, 2, N_MEM])
        vm = sb("vm", [P, MB, HW])
        w_hi = sb("wo_hi", [P, KC, D], F32R)
        w_lo = sb("wo_lo", [P, KC, D], F32R)
        level_mask = sb("level_mask", [P, NL, GLA_H * P // 2])
        eye = sb("eye", [P, GLA_H * P])
        prepare(nc, projT, mem, w_mem_kv, w_alpha2, b_alpha, w_out, gsum, kmT, vm, w_hi, w_lo, level_mask, eye, ident)
        mix_and_project(nc, x, sb_out, projT, gla_norm_w, ln_g, ln_b, gsum, kmT, vm, w_hi, w_lo, level_mask, eye, ident, out)


def hybrid_layer(nc, x, mem, w_in, w_alpha2, b_alpha, gla_norm_w, w_mem_kv, w_out, ln_g, ln_b, out):
    projT = nc.dram_tensor("projT", (D_IN, T), F32).ap()
    sb_out = nc.dram_tensor("sb_out", (T, SB_H * DH), F32).ap()
    with ExitStack() as ctx:
        ident = ctx.enter_context(nc.sbuf_tensor("ident", [P, P], F32))
        make_identity(nc, ident)
        project(nc, x, w_in, projT, ident)
        stick_breaking(nc, projT, sb_out, ident)
        last_stage(nc, x, mem, w_alpha2, b_alpha, gla_norm_w, w_mem_kv, w_out, ln_g, ln_b, sb_out, projT, ident, out)


INPUTS = ["x", "mem", "w_in", "w_alpha2", "b_alpha", "gla_norm_w", "w_mem_kv", "w_out", "ln_g", "ln_b"]


def kernel(**inputs):
    import numpy as np
    import concourse.bacc as bacc
    from concourse.bass_utils import run_bass_kernel_spmd

    nc = bacc.Bacc("TRN2", target_bir_lowering=False, num_devices=1)
    arrays, args = {}, []
    for name in INPUTS:
        a = np.ascontiguousarray(inputs[name])
        arrays[f"in_{name}"] = a
        args.append(nc.dram_tensor(f"in_{name}", a.shape, mybir.dt.from_np(a.dtype), kind="ExternalInput").ap())
    out = nc.dram_tensor("out", (1, T, D), F32, kind="ExternalOutput").ap()
    hybrid_layer(nc, *args, out)
    result = run_bass_kernel_spmd(nc, [arrays], core_ids=[0])
    return result.results[0]["out"]
```
